# Optimizing a Trainium2 kernel written in Bass

```python
import math
import jax, jax.numpy as jnp
from jax import lax
import numpy as np

D_MODEL = 2048
BATCH = 1
SEQ = 512
DEPTH = 1
DEC_BATCH = 8
DEC_SEQ = 16
PAST_LEN = 256

CHUNK = 64
GLA_HEADS = 4
GLA_DK = D_MODEL // 2
GLA_DV = D_MODEL
GLA_DK_HEAD = GLA_DK // GLA_HEADS
GLA_DV_HEAD = GLA_DV // GLA_HEADS
GLA_GATE_RANK = 16
GLA_GATE_NORM = 16.0
CONV_CH = D_MODEL // 2
CONV_WIDTH = 31
PEER_HEADS = 8
PEER_NKEYS = 128
PEER_EXPERTS = PEER_NKEYS * PEER_NKEYS
PEER_DQ = 256
PEER_DQ_HALF = PEER_DQ // 2
PEER_TOPK = 16
PEER_BLOCK = 128
EPS = 1e-6
IN_WIDTHS = (GLA_DK, GLA_DK, GLA_DV, GLA_DV, GLA_GATE_RANK, 2 * CONV_CH, D_MODEL, D_MODEL)
D_IN = GLA_DK * 2 + GLA_DV * 2 + GLA_GATE_RANK + 2 * CONV_CH + 2 * D_MODEL

kernel_name = 'hybrid_gla_conformer_peer_stream_step'

def rms_norm(x, g):
    xf = x.astype(jnp.float32)
    y = xf * lax.rsqrt(jnp.mean(xf * xf, axis=-1, keepdims=True) + EPS)
    return (y * g.astype(jnp.float32)).astype(x.dtype)

def layer_norm(x, g, b):
    xf = x.astype(jnp.float32)
    mu = jnp.mean(xf, axis=-1, keepdims=True)
    xc = xf - mu
    y = xc * lax.rsqrt(jnp.mean(xc * xc, axis=-1, keepdims=True) + EPS)
    return (y * g.astype(jnp.float32) + b.astype(jnp.float32)).astype(x.dtype)

def gla_chunked(q, k, v, log_a, s0):
    B, T, H, Dk = q.shape
    Dv = v.shape[-1]
    L = min(CHUNK, T)
    n = T // L

    def to_chunks(a):
        return jnp.moveaxis(a.astype(jnp.float32).reshape(B, n, L, H, a.shape[-1]), 1, 0)

    mask = jnp.tril(jnp.ones((L, L), dtype=bool))

    def step(S, inp):
        qc, kc, vc, lac = inp
        b = jnp.cumsum(lac, axis=1)
        b_last = b[:, -1]
        q_in = qc * jnp.exp(b)
        k_in = kc * jnp.exp(-b)
        k_out = kc * jnp.exp(b_last[:, None] - b)
        att = jnp.where(mask, jnp.einsum('bthk,bshk->bhts', q_in, k_in), 0.0)
        o = jnp.einsum('bhts,bshv->bthv', att, vc) + jnp.einsum('bthk,bhkv->bthv', q_in, S)
        S = jnp.exp(b_last)[..., None] * S + jnp.einsum('bshk,bshv->bhkv', k_out, vc)
        return S, o

    S, o = lax.scan(step, s0.astype(jnp.float32),
                    (to_chunks(q), to_chunks(k), to_chunks(v), to_chunks(log_a)))
    o = jnp.moveaxis(o, 0, 1).reshape(B, T, H, Dv)
    return o, S

def conformer_conv(zc, buf, w_dw, b_dw, g_ln, b_ln, w_o):
    a, g = jnp.split(zc, 2, axis=-1)
    u = a * jax.nn.sigmoid(g)
    full = jnp.concatenate([buf.astype(u.dtype), u], axis=1)
    y = lax.conv_general_dilated(full, w_dw.astype(full.dtype)[:, None, :], window_strides=(1,),
                                 padding='VALID', dimension_numbers=('NWC', 'WIO', 'NWC'),
                                 feature_group_count=CONV_CH) + b_dw
    new_buf = full[:, -(CONV_WIDTH - 1):]
    y = jax.nn.silu(layer_norm(y, g_ln, b_ln))
    return y @ w_o, new_buf

def peer(h, w_pq, k_sub1, k_sub2, u_exp, v_exp):
    B, T, D = h.shape
    x = h.reshape(B * T, D)
    N = x.shape[0]
    q = (x @ w_pq).astype(jnp.float32).reshape(N, PEER_HEADS, 2, PEER_DQ_HALF)
    s1 = jnp.einsum('nhd,kd->nhk', q[:, :, 0], k_sub1.astype(jnp.float32))
    s2 = jnp.einsum('nhd,kd->nhk', q[:, :, 1], k_sub2.astype(jnp.float32))
    v1, i1 = lax.top_k(s1, PEER_TOPK)
    v2, i2 = lax.top_k(s2, PEER_TOPK)
    cand = (v1[..., :, None] + v2[..., None, :]).reshape(N, PEER_HEADS, PEER_TOPK * PEER_TOPK)
    cidx = (i1[..., :, None] * PEER_NKEYS + i2[..., None, :]).reshape(N, PEER_HEADS, PEER_TOPK * PEER_TOPK)
    sc, pos = lax.top_k(cand, PEER_TOPK)
    idx = jnp.take_along_axis(cidx, pos, axis=-1)
    wts = jax.nn.softmax(sc, axis=-1)
    pad = (-N) % PEER_BLOCK
    xp = jnp.pad(x, ((0, pad), (0, 0)))
    ip = jnp.pad(idx, ((0, pad), (0, 0), (0, 0)))
    wp = jnp.pad(wts, ((0, pad), (0, 0), (0, 0)))
    nb = (N + pad) // PEER_BLOCK

    def block(args):
        xb, ib, wb = args
        ub = jnp.take(u_exp, ib, axis=0)
        act = jax.nn.gelu(jnp.einsum('nhed,nd->nhe', ub, xb).astype(jnp.float32), approximate=False)
        vb = jnp.take(v_exp, ib, axis=0)
        return jnp.einsum('nhe,nhed->nd', wb * act, vb.astype(jnp.float32))

    out = lax.map(block, (xp.reshape(nb, PEER_BLOCK, D),
                          ip.reshape(nb, PEER_BLOCK, PEER_HEADS, PEER_TOPK),
                          wp.reshape(nb, PEER_BLOCK, PEER_HEADS, PEER_TOPK)))
    return out.reshape(nb * PEER_BLOCK, D)[:N].reshape(B, T, D).astype(h.dtype)

def hybrid_layer(x, c, s_gla, buf_conv, w_ada, b_ada, g_pre_mix, g_post_mix, w_in, w_alpha_up, b_alpha,
                 g_gla_out, w_gla_o, w_dw, b_dw, g_conv_ln, b_conv_ln, w_conv_o, w_out,
                 g_pre_ffn, g_post_ffn, w_pq, k_sub1, k_sub2, u_exp, v_exp):
    B, T, _ = x.shape
    mod = jax.nn.silu(c) @ w_ada + b_ada
    sh1, sc1, gt1, sh2, sc2, gt2 = [m[:, None, :] for m in jnp.split(mod, 6, axis=-1)]

    h = rms_norm(x, g_pre_mix) * (1 + sc1) + sh1
    z = h @ w_in
    split_pts = np.cumsum(IN_WIDTHS)[:-1].tolist()
    zq, zk, zv, zr, zlr, zc, zga, zgb = jnp.split(z, split_pts, axis=-1)

    q = zq.reshape(B, T, GLA_HEADS, GLA_DK_HEAD) * (GLA_DK_HEAD ** -0.5)
    k = zk.reshape(B, T, GLA_HEADS, GLA_DK_HEAD)
    v = zv.reshape(B, T, GLA_HEADS, GLA_DV_HEAD)
    log_a = jax.nn.log_sigmoid((zlr @ w_alpha_up + b_alpha).astype(jnp.float32)) / GLA_GATE_NORM
    log_a = log_a.reshape(B, T, GLA_HEADS, GLA_DK_HEAD)
    o, s_new = gla_chunked(q, k, v, log_a, s_gla)
    o = rms_norm(o, g_gla_out).reshape(B, T, GLA_DV) * jax.nn.silu(zr.astype(jnp.float32))
    y_a = o.astype(x.dtype) @ w_gla_o

    y_b, buf_new = conformer_conv(zc, buf_conv, w_dw, b_dw, g_conv_ln, b_conv_ln, w_conv_o)

    mix = (jax.nn.sigmoid(zga) * y_a + jax.nn.sigmoid(zgb) * y_b) @ w_out
    x = x + gt1 * rms_norm(mix, g_post_mix)

    h2 = rms_norm(x, g_pre_ffn) * (1 + sc2) + sh2
    f = peer(h2, w_pq, k_sub1, k_sub2, u_exp, v_exp)
    x = x + gt2 * rms_norm(f, g_post_ffn)
    return x, s_new, buf_new

def setup_inputs(seed: int = 0) -> dict:
    key = jax.random.key(seed)
    ks = jax.random.split(key, 32)
    D = D_MODEL
    L = DEPTH

    def nrm(k, shape, s):
        return jax.random.normal(k, shape, jnp.float32) * s

    return {
        'x_prompt': nrm(ks[0], (BATCH, SEQ, D), 1.0),
        'x_sample': nrm(ks[1], (DEC_BATCH, DEC_SEQ, D), 1.0),
        'state_gla': nrm(ks[2], (L, DEC_BATCH, GLA_HEADS, GLA_DK_HEAD, GLA_DV_HEAD), 0.1),
        'cache_conv': nrm(ks[3], (L, DEC_BATCH, CONV_WIDTH - 1, CONV_CH), 0.5),
        'c_prompt': nrm(ks[4], (BATCH, D), 1.0),
        'c_sample': nrm(ks[5], (DEC_BATCH, D), 1.0),
        'w_ada': nrm(ks[6], (L, D, 6 * D), 0.5 * D ** -0.5),
        'b_ada': nrm(ks[7], (L, 6 * D), 0.02),
        'g_pre_mix': 1.0 + nrm(ks[8], (L, D), 0.02),
        'g_post_mix': 1.0 + nrm(ks[9], (L, D), 0.02),
        'w_in': nrm(ks[10], (L, D, D_IN), D ** -0.5),
        'w_alpha_up': nrm(ks[11], (L, GLA_GATE_RANK, GLA_DK), GLA_GATE_RANK ** -0.5),
        'b_alpha': nrm(ks[12], (L, GLA_DK), 0.1),
        'g_gla_out': 1.0 + nrm(ks[13], (L, GLA_DV_HEAD), 0.02),
        'w_gla_o': nrm(ks[14], (L, GLA_DV, D), GLA_DV ** -0.5),
        'w_dw': nrm(ks[15], (L, CONV_WIDTH, CONV_CH), CONV_WIDTH ** -0.5),
        'b_dw': nrm(ks[16], (L, CONV_CH), 0.02),
        'g_conv_ln': 1.0 + nrm(ks[17], (L, CONV_CH), 0.02),
        'b_conv_ln': nrm(ks[18], (L, CONV_CH), 0.02),
        'w_conv_o': nrm(ks[19], (L, CONV_CH, D), CONV_CH ** -0.5),
        'w_out': nrm(ks[20], (L, D, D), D ** -0.5),
        'g_pre_ffn': 1.0 + nrm(ks[21], (L, D), 0.02),
        'g_post_ffn': 1.0 + nrm(ks[22], (L, D), 0.02),
        'w_pq': nrm(ks[23], (L, D, PEER_HEADS * PEER_DQ), D ** -0.5),
        'k_sub1': nrm(ks[24], (L, PEER_NKEYS, PEER_DQ_HALF), PEER_DQ_HALF ** -0.5),
        'k_sub2': nrm(ks[25], (L, PEER_NKEYS, PEER_DQ_HALF), PEER_DQ_HALF ** -0.5),
        'u_exp': nrm(ks[26], (L, PEER_EXPERTS, D), D ** -0.5),
        'v_exp': nrm(ks[27], (L, PEER_EXPERTS, D), 0.25),
    }

def reference(x_prompt, x_sample, state_gla, cache_conv, c_prompt, c_sample, w_ada, b_ada, g_pre_mix,
              g_post_mix, w_in, w_alpha_up, b_alpha, g_gla_out, w_gla_o, w_dw, b_dw, g_conv_ln, b_conv_ln,
              w_conv_o, w_out, g_pre_ffn, g_post_ffn, w_pq, k_sub1, k_sub2, u_exp, v_exp):
    params = (w_ada, b_ada, g_pre_mix, g_post_mix, w_in, w_alpha_up, b_alpha, g_gla_out, w_gla_o, w_dw,
              b_dw, g_conv_ln, b_conv_ln, w_conv_o, w_out, g_pre_ffn, g_post_ffn, w_pq, k_sub1, k_sub2,
              u_exp, v_exp)
    xp, xs = x_prompt, x_sample
    bp = xp.shape[0]
    sg_p, cb_p, sg_s, cb_s = [], [], [], []
    for l in range(DEPTH):
        pl = [p[l] for p in params]
        s0 = jnp.zeros((bp, GLA_HEADS, GLA_DK_HEAD, GLA_DV_HEAD), jnp.float32)
        buf0 = jnp.zeros((bp, CONV_WIDTH - 1, CONV_CH), xp.dtype)
        xp, s_p, b_p = hybrid_layer(xp, c_prompt, s0, buf0, *pl)
        xs, s_s, b_s = hybrid_layer(xs, c_sample, state_gla[l], cache_conv[l], *pl)
        sg_p.append(s_p)
        cb_p.append(b_p)
        sg_s.append(s_s)
        cb_s.append(b_s)
    return (xp, xs, jnp.stack(sg_p), jnp.stack(cb_p), jnp.stack(sg_s), jnp.stack(cb_s))


_drawn_inputs = setup_inputs


def setup_inputs(seed=0):
    import zlib

    import numpy as np

    out = dict(_drawn_inputs(seed))
    spreads = {}
    factors = {'g_gla_out': 2.719, 'b_conv_ln': 2.904, 'g_post_ffn': 8.0}
    for name, (base, spread) in spreads.items():
        noise = np.random.default_rng([zlib.crc32(name.encode()), seed]).standard_normal(out[name].shape)
        drawn = base * np.exp(spread * noise) if base else spread * noise
        out[name] = __import__('jax').numpy.asarray(drawn.astype(out[name].dtype))
    for name, factor in factors.items():
        out[name] = (out[name] * factor).astype(out[name].dtype)
    return out
```

```python
from contextlib import ExitStack, contextmanager

import numpy as np

import concourse.bass as bass
from concourse import mybir

F32 = mybir.dt.float32
F32R = mybir.dt.float32r
U32 = mybir.dt.uint32
ALU = mybir.AluOpType
ACT = mybir.ActivationFunctionType
AX = mybir.AxisListType

P = 128
D = 2048
NP_TOK = 512
STREAMS = 8
ST_TOK = 16
NTOK = NP_TOK + STREAMS * ST_TOK
TT = NTOK // P
TP = NP_TOK // P
KD = D // P
NSEQ = 1 + STREAMS
CHUNK = 64
HEADS = 4
DKH = 256
DVH = 512
DK = HEADS * DKH
DV = HEADS * DVH
RANK = 16
CC = 1024
CT = CC // P
TAPS = 31
HIST = TAPS - 1
PH = 8
NKEY = 128
TOPK = 16
SLOTS = PH * TOPK
EPS = 1e-6
GATE_NORM = 16.0
NCOL = 512
QK = 4
QPC = KD // QK

C_Q, C_K, C_V, C_R = 0, DK, 2 * DK, 2 * DK + DV
C_LR = C_R + DV
C_A = C_LR + RANK
C_G = C_A + CC
C_GA = C_G + CC
C_GB = C_GA + D

K_ID, K_CUMP, K_RESTP, K_CUMS, K_RESTS, K_ONES, K_IOTA = (P * n for n in range(7))
K_INDP = 7 * P
K_INDS = K_INDP + 2
K_END = K_INDS + STREAMS


def constants():
    k = np.zeros((P, K_END), np.float32)
    s, t = np.arange(P)[:, None], np.arange(P)[None, :]
    k[:, K_ID:K_ID + P] = s == t
    for at_cum, at_rest, size in ((K_CUMP, K_RESTP, CHUNK), (K_CUMS, K_RESTS, ST_TOK)):
        same = s // size == t // size
        k[:, at_cum:at_cum + P] = same & (s <= t)
        k[:, at_rest:at_rest + P] = same & (s > t)
    k[:, K_ONES:K_ONES + P] = 1.0
    k[:, K_IOTA:K_IOTA + P] = t
    k[:, K_INDP:K_INDP + 2] = s // CHUNK == np.arange(2)[None, :]
    k[:, K_INDS:K_INDS + STREAMS] = s // ST_TOK == np.arange(STREAMS)[None, :]
    spread = np.zeros((NSEQ, NTOK), np.float32)
    spread[0, :NP_TOK] = 1.0
    for j in range(STREAMS):
        spread[1 + j, NP_TOK + ST_TOK * j:NP_TOK + ST_TOK * (j + 1)] = 1.0
    return k, spread


class Link:

    def __init__(self, eng, sem):
        self.eng, self.sem, self.base, self.n = eng, sem, 0, 0

    def mark(self, ins):
        ins.then_inc(self.sem, 1)
        self.n += 1
        return ins

    def sync(self, back=0):
        self.eng.wait_ge(self.sem, self.base + (self.n - back))

    def enter(self, i, per):
        self.outer, self.before = (self.base, self.n), self.base + self.n
        self.base, self.n, self.per = i * per + self.before, 0, per

    def leave_step(self):
        assert self.n == self.per, (self.n, self.per)

    def leave(self, steps):
        self.base, self.n = self.before + steps * self.per, 0


def build(nc, a):
    stack = ExitStack()
    with stack:
        _build(nc, a, stack)


def _build(nc, a, stack):
    stage_sems = []

    def sem(name):
        stage_sems.append(nc.alloc_semaphore(name))
        return stage_sems[-1]

    @contextmanager
    def stage():
        before = len(stage_sems)
        with ExitStack() as st, nc.Block() as block:
            yield st, block
        nc.clear_and_free_semaphores(stage_sems[before:])
        del stage_sems[before:]
        nc.all_engine_barrier()

    def dram(name, shape, dt=F32):
        return nc.dram_tensor(name, shape, dt).ap()

    def sb(st, name, shape, dt=F32):
        return st.enter_context(nc.sbuf_tensor(name, shape, dt))

    d_mod = dram("d_mod", (NSEQ, 6 * D))
    d_qin, d_kin, d_kout = (dram(n, (NTOK, DK)) for n in ("d_qin", "d_kin", "d_kout"))
    d_v, d_r = dram("d_v", (NTOK, DV)), dram("d_r", (NTOK, DV))
    d_gates = dram("d_gates", (NTOK, 2 * D))
    d_u = dram("d_u", (NTOK, CC))
    d_o = dram("d_o", (NTOK, DV))
    d_mb, d_m, d_mix = (dram(n, (NTOK, D)) for n in ("d_mb", "d_m", "d_mix"))
    d_x2, d_h2, d_q = (dram(n, (NTOK, D)) for n in ("d_x2", "d_h2", "d_q"))
    d_decay = dram("d_decay", (P, DK // P, 2 * TP + STREAMS))

    kc = sb(stack, "kc", [P, K_END])
    main_scope = stack.enter_context(ExitStack())
    act_hi = sb(main_scope, "act_hi", [P, KD, NTOK], F32R)
    act_lo = sb(main_scope, "act_lo", [P, KD, NTOK], F32R)
    w_in_st = sb(main_scope, "w_stage", [P, QPC, QK, NCOL])
    w_hi = sb(main_scope, "w_hi", [P, 2, QK, NCOL], F32R)
    w_lo = sb(main_scope, "w_lo", [P, 2, QK, NCOL], F32R)
    ps = stack.enter_context(nc.psum_tensor("ps", [P, 8, NCOL], F32))
    ident = kc[:, K_ID:K_ID + P]

    w_landed = [sem(f"w_landed{q}") for q in range(QPC)]
    w_hi_done = sem("w_hi_done")
    w_split = sem("w_split")
    w_used = sem("w_used")
    acc_done = sem("acc_done")
    bank_free = sem("bank_free")
    s_const = sem("s_const")
    l_act, l_dve, l_pool = sem("l_act"), sem("l_dve"), sem("l_pool")
    t_ready = sem("t_ready")
    t_taken = sem("t_taken")
    t_hi = sem("t_hi")
    store_gate = sem("store_gate")
    links = {}

    def link(eng, name):
        if name not in links:
            links[name] = Link(eng, {"act": l_act, "dve": l_dve, "pool": l_pool}[name])
        links[name].eng = eng
        return links[name]

    def load_quarter(sp, c, q, src):
        sp.wait_ge(w_split, c * QPC + (q + 1))
        sp.dma_start(w_in_st[:, q], src).then_inc(w_landed[q], 16)

    def split_hi(act, c, q, sums):
        act.wait_ge(w_landed[q], c * 16 + 16)
        if q == 1:
            act.wait_ge(acc_done, sums)
        else:
            act.wait_ge(w_used, c * (QPC - 1) + max(q, 1))
        act.activation(w_hi[:, q % 2], w_in_st[:, q], ACT.Copy).then_inc(w_hi_done, 1)

    def split_lo(dve, c, q):
        dve.wait_ge(w_hi_done, c * QPC + (q + 1))
        dve.tensor_tensor(w_lo[:, q % 2], w_in_st[:, q], w_hi[:, q % 2].bitcast(F32),
                          ALU.subtract).then_inc(w_split, 1)

    def product(pe, out, lhs, rhs, first, last):
        pe.matmul(out, lhs[0], rhs[0], start=first, stop=False)
        pe.matmul(out, lhs[0], rhs[1], start=False, stop=False)
        return pe.matmul(out, lhs[1], rhs[0], start=False, stop=last)

    def multiply_chunk(pe, c, g, quarters=QPC, q0=0, between=None):
        for q in range(quarters):
            pe.wait_ge(w_split, c * QPC + (q0 + q + 1 + QPC))
            for t in range(TT):
                if q == 0:
                    pe.wait_ge(bank_free, g * TT + (t + 1))
                for kk in range(QK):
                    k = q * QK + kk
                    at = (slice(None), k, slice(t * P, t * P + P))
                    mm = product(pe, ps[:, t], (act_hi[at], act_lo[at]),
                                 (w_hi[:, (q0 + q) % 2, kk], w_lo[:, (q0 + q) % 2, kk]),
                                 k == 0, k == quarters * QK - 1)
                if q == quarters - 1:
                    mm.then_inc(acc_done, 1)
            if q < quarters - 1:
                mm.then_inc(w_used, 1)
            if between:
                between(q)

    def rows(w, col, q):
        return w[q * QK * P:(q + 1) * QK * P, bass.ds(col, NCOL)].rearrange("(k p) n -> p k n", p=P)

    NA = 6 * D // NCOL
    with stage() as (st, block):
        c_in = sb(st, "c_in", [P, KD, NSEQ])
        c_sig = sb(st, "c_sig", [P, KD, NSEQ])
        c_hi = sb(st, "c_hi", [P, KD, NSEQ + 1], F32R)
        c_lo = sb(st, "c_lo", [P, KD, NSEQ + 1], F32R)
        mod = sb(st, "mod", [NSEQ, 6 * D])
        s_c, s_b, s_csplit, s_modout = sem("s_c"), sem("s_b"), sem("s_csplit"), sem("s_modout")
        s_csig = sem("s_csig")
        mod_read = sem("mod_read")

        @block.sync
        def _(sp):
            sp.dma_start(c_in[:], a["cT"]).then_inc(s_c, 16)
            with sp.Fori(0, NA) as c:
                for q in range(QPC):
                    load_quarter(sp, c, q, rows(a["w_ada"], c * NCOL, q))

        @block.gpsimd
        def _(pool):
            pool.dma_start(kc[:], a["consts"]).then_inc(s_const, 16)
            pool.dma_start(mod[:], a["b_ada"].broadcast_to([NSEQ, 6 * D])).then_inc(s_b, 16)
            pool.wait_ge(s_const, 16)
            pool.wait_ge(mod_read, NA + 1)
            pool.dma_start(d_mod, mod[:]).then_inc(s_modout, 16)
            pool.wait_ge(s_modout, 16)

        @block.scalar
        def _(act):
            act.sem_inc(w_split, QPC)
            act.wait_ge(s_c, 16)
            act.activation(c_sig[:], c_in[:], ACT.Sigmoid).then_inc(s_csig, 1)
            with act.Fori(0, NA) as c:
                for q in range(QPC):
                    split_hi(act, c, q, c + 1)

        @block.vector
        def _(dve):
            lk = link(dve, "dve")
            lk.mark(dve.memset(c_hi[:].bitcast(F32), 0.0))
            lk.mark(dve.memset(c_lo[:].bitcast(F32), 0.0))
            dve.wait_ge(s_csig, 1)
            lk.mark(dve.tensor_tensor(c_in[:], c_in[:], c_sig[:], ALU.mult))
            lk.sync()
            lk.mark(dve.tensor_copy(c_hi[:, :, 0:NSEQ], c_in[:]))
            lk.sync()
            dve.tensor_tensor(c_lo[:, :, 0:NSEQ], c_in[:], c_hi[:, :, 0:NSEQ].bitcast(F32),
                              ALU.subtract).then_inc(s_csplit, 1)
            dve.wait_ge(s_b, 16)
            split_lo(dve, 0, 0)
            with dve.Fori(0, NA - 1) as c:
                for q in range(1, QPC):
                    split_lo(dve, c, q)
                split_lo(dve, c + 1, 0)
                dve.wait_ge(acc_done, c + 2)
                m = mod[:, bass.ds(c * NCOL, NCOL)]
                dve.tensor_tensor(m, m, ps[0:NSEQ, 0], ALU.add).then_inc(mod_read, 1)
            for q in range(1, QPC):
                split_lo(dve, NA - 1, q)
            dve.wait_ge(acc_done, NA + 1)
            m = mod[:, (NA - 1) * NCOL:NA * NCOL]
            dve.tensor_tensor(m, m, ps[0:NSEQ, 0], ALU.add).then_inc(mod_read, 1)

        @block.tensor
        def _(pe):
            pe.sem_inc(w_used, 1)
            pe.sem_inc(acc_done, 1)
            pe.sem_inc(bank_free, TT)
            pe.sem_inc(mod_read, 1)
            pe.wait_ge(s_csplit, 1)
            with pe.Fori(0, NA) as c:
                for q in range(QPC):
                    pe.wait_ge(w_split, c * QPC + (q + 1 + QPC))
                    if q == 0:
                        pe.wait_ge(mod_read, c + 1)
                    for kk in range(QK):
                        k = q * QK + kk
                        mm = product(pe, ps[0:NSEQ + 1, 0], (c_hi[:, k], c_lo[:, k]),
                                     (w_hi[:, q % 2, kk], w_lo[:, q % 2, kk]), k == 0, k == KD - 1)
                    if q < QPC - 1:
                        mm.then_inc(w_used, 1)
                mm.then_inc(acc_done, 1)
    chunks = NA
    sums = 0
    acc_base = 1 + NA

    t_count = [0]

    def transpose_group(pe, G, g, src):
        pe.wait_ge(t_taken, G + 1)
        for j in range(4):
            mm = pe.transpose(ps[:, 4 + g, j * P:(j + 1) * P], src[:, j * P:(j + 1) * P], ident)
        mm.then_inc(t_ready, 1)

    def take_hi(act, G, g, t):
        act.wait_ge(t_ready, G + 1)
        act.activation(act_hi[:, 4 * g:4 * g + 4, bass.ds(t * P, P)],
                       ps[:, 4 + g].rearrange("p (j n) -> p j n", j=4), ACT.Copy).then_inc(t_hi, 1)

    def take_lo(dve, G, g, t):
        dve.wait_ge(t_hi, G + 1)
        dve.tensor_tensor(act_lo[:, 4 * g:4 * g + 4, bass.ds(t * P, P)],
                          ps[:, 4 + g].rearrange("p (j n) -> p j n", j=4),
                          act_hi[:, 4 * g:4 * g + 4, bass.ds(t * P, P)].bitcast(F32),
                          ALU.subtract).then_inc(t_taken, 1)

    def norm_stage(name, src, col_shift, col_scale, g_row, G0, credit, residual=None):
        with stage() as (st, block):
            xt = sb(st, name + "_x", [P, D])
            ht = sb(st, name + "_h", [P, D])
            gain = sb(st, name + "_gain", [NSEQ, D])
            shift = sb(st, name + "_shift", [NSEQ, D])
            g9 = ht[0:NSEQ]
            rowsel = sb(st, name + "_rowsel", [NSEQ, P])
            ss = sb(st, name + "_ss", [P, 8])
            if residual is not None:
                post = sb(st, name + "_post", [NSEQ, D])
                xr = sb(st, name + "_xr", [P, D])
                gp = xt[0:NSEQ]
                s_xr, s_mss, s_mvar, s_mstd, s_x2, s_kept, xr_free = (
                    sem(name + n) for n in ("_xr", "_mss", "_mvar", "_mstd", "_x2", "_kept", "_xrfree"))
            s_mod, s_x = sem(name + "_mod"), sem(name + "_x")
            s_gain, s_ss, s_var, s_std = (sem(name + n) for n in ("_gain", "_ss", "_var", "_std"))
            e_ready = sem(name + "_eready")
            h_ready = sem(name + "_hready")

            n_e = 8 if residual is None else 12

            @block.sync
            def _(sp):
                sp.dma_start(gain[:], d_mod[:, col_scale:col_scale + D]).then_inc(s_mod, 16)
                sp.dma_start(shift[:], d_mod[:, col_shift:col_shift + D]).then_inc(s_mod, 16)
                sp.dma_start(g9, g_row.broadcast_to([NSEQ, D])).then_inc(s_mod, 16)
                if residual is not None:
                    sp.dma_start(post[:], d_mod[:, 2 * D:3 * D]).then_inc(s_mod, 16)
                    sp.dma_start(gp, a["g_post_mix"].broadcast_to([NSEQ, D])).then_inc(s_mod, 16)
                    sp.wait_ge(s_gain, 2)
                with sp.Fori(0, TT) as t:
                    if residual is None:
                        sp.wait_ge(h_ready, t * 4 + 2)
                    else:
                        sp.wait_ge(xr_free, t + 1)
                        sp.dma_start(xr[:], residual[bass.ds(t * P, P), :]).then_inc(s_xr, 16)
                    sp.dma_start(xt[:], src[bass.ds(t * P, P), :]).then_inc(s_x, 16)
                    sp.dma_start(rowsel[:], a["spread"][:, bass.ds(t * P, P)]).then_inc(s_x, 16)

            @block.scalar
            def _(act):
                if credit:
                    act.sem_inc(t_taken, 4)
                act.sem_inc(h_ready, 2)
                act.wait_ge(s_gain, 1 if residual is None else 2)
                with act.Fori(0, TT) as t:
                    act.wait_ge(s_x, t * 32 + 32)
                    act.wait_ge(t_taken, t * 4 + (G0 + 4))
                    if residual is not None:
                        act.wait_ge(xr_free, t + 1)
                        act.activation(ht[:], xt[:], ACT.Square, accum_out=ss[:, 4:5]).then_inc(s_mss, 1)
                        act.wait_ge(s_mvar, t + 1)
                        act.activation(ss[:, 6:7], ss[:, 5:6], ACT.Sqrt).then_inc(s_mstd, 1)
                        act.wait_ge(s_x2, t * 4 + 4)
                    act.activation(ht[:], xt[:], ACT.Square, accum_out=ss[:, 0:1]).then_inc(s_ss, 1)
                    act.wait_ge(s_var, t + 1)
                    act.activation(ss[:, 2:3], ss[:, 1:2], ACT.Sqrt).then_inc(s_std, 1)
                    for g in range(4):
                        take_hi(act, t * 4 + (G0 + g), g, t)

            @block.vector
            def _(dve):
                lk = link(dve, "dve")
                dve.wait_ge(s_mod, 48 if residual is None else 80)
                dve.scalar_tensor_tensor(out=gain[:], in0=gain[:], scalar=1.0, in1=g9,
                                         op0=ALU.add, op1=ALU.mult).then_inc(s_gain, 1)
                if residual is not None:
                    dve.tensor_tensor(post[:], post[:], gp, ALU.mult).then_inc(s_gain, 1)
                with dve.Fori(0, TT) as t:
                    lk.enter(t, 5 + (5 if residual is not None else 0))
                    if residual is not None:
                        dve.wait_ge(s_mss, t + 1)
                        dve.tensor_scalar(ss[:, 5:6], ss[:, 4:5], 1.0 / D, EPS, ALU.mult, ALU.add).then_inc(s_mvar, 1)
                        dve.wait_ge(s_mstd, t + 1)
                        lk.mark(dve.reciprocal(ss[:, 7:8], ss[:, 6:7]))
                        lk.sync()
                        dve.wait_ge(s_xr, t * 16 + 16)
                        for g in range(4):
                            cols = slice(g * NCOL, (g + 1) * NCOL)
                            dve.wait_ge(e_ready, t * n_e + (g + 1))
                            lk.mark(dve.scalar_tensor_tensor(out=xt[:, cols], in0=xt[:, cols], scalar=ss[:, 7:8],
                                                             in1=ps[:, g % 4], op0=ALU.mult, op1=ALU.mult))
                            lk.sync()
                            dve.tensor_tensor(xt[:, cols], xt[:, cols], xr[:, cols], ALU.add).then_inc(s_x2, 1)
                        dve.wait_ge(s_x2, t * 4 + 4)
                    dve.wait_ge(s_ss, t + 1)
                    dve.tensor_scalar(ss[:, 1:2], ss[:, 0:1], 1.0 / D, EPS, ALU.mult, ALU.add).then_inc(s_var, 1)
                    dve.wait_ge(s_std, t + 1)
                    lk.mark(dve.reciprocal(ss[:, 3:4], ss[:, 2:3]))
                    lk.sync()
                    for g in range(4):
                        cols = slice(g * NCOL, (g + 1) * NCOL)
                        dve.wait_ge(e_ready, t * n_e + (n_e - 8 + 2 * g + 1))
                        lk.mark(dve.scalar_tensor_tensor(out=ht[:, cols], in0=xt[:, cols], scalar=ss[:, 3:4],
                                                         in1=ps[:, g % 2], op0=ALU.mult, op1=ALU.mult))
                        dve.wait_ge(e_ready, t * n_e + (n_e - 8 + 2 * g + 2))
                        lk.sync()
                        dve.tensor_tensor(ht[:, cols], ht[:, cols], ps[:, 2 + g % 2], ALU.add).then_inc(h_ready, 1)
                        if g > 0:
                            take_lo(dve, t * 4 + (G0 + g - 1), g - 1, t)
                    take_lo(dve, t * 4 + (G0 + 3), 3, t)
                    lk.leave_step()
                lk.leave(TT)

            if residual is not None:
                @block.gpsimd
                def _(pool):
                    pool.sem_inc(xr_free, 1)
                    with pool.Fori(0, TT) as t:
                        pool.wait_ge(s_x2, t * 4 + 4)
                        pool.sem_inc(store_gate, 1)
                        pool.dma_start(d_x2[bass.ds(t * P, P), :], xt[:]).then_inc(s_kept, 16)
                        pool.wait_ge(h_ready, t * 4 + 6)
                        pool.sem_inc(store_gate, 1)
                        pool.dma_start(d_h2[bass.ds(t * P, P), :], ht[:]).then_inc(s_kept, 16)
                        pool.wait_ge(s_kept, t * 32 + 32)
                        pool.sem_inc(xr_free, 1)

            @block.tensor
            def _(pe):
                pe.wait_ge(s_gain, 1 if residual is None else 2)
                with pe.Fori(0, TT) as t:
                    pe.wait_ge(s_x, t * 32 + 32)
                    if residual is not None:
                        pe.wait_ge(h_ready, t * 4 + 2)
                        for g in range(4):
                            pe.matmul(ps[:, g], rowsel[:], post[:, g * NCOL:(g + 1) * NCOL], start=True,
                                      stop=True).then_inc(e_ready, 1)
                        pe.wait_ge(s_x2, t * 4 + 4)
                    for g in range(4):
                        cols = slice(g * NCOL, (g + 1) * NCOL)
                        pe.wait_ge(h_ready, t * 4 + (g + 1))
                        pe.matmul(ps[:, g % 2], rowsel[:], gain[:, cols], start=True, stop=True).then_inc(e_ready, 1)
                        pe.matmul(ps[:, 2 + g % 2], rowsel[:], shift[:, cols], start=True, stop=True).then_inc(e_ready, 1)
                    for g in range(4):
                        pe.wait_ge(h_ready, t * 4 + (g + 3))
                        transpose_group(pe, t * 4 + (G0 + g), g, ht[:, g * NCOL:(g + 1) * NCOL])

    norm_stage("n1", a["x"], 0, D, a["g_pre_mix"], 0, True)
    t_groups = 4 * TT

    NHALF = DK // NCOL
    c_q0 = NA
    c_v0 = c_q0 + 2 * NHALF
    c_u0 = c_v0 + DV // NCOL
    c_r0 = c_u0 + 2 * (CC // NCOL)
    c_g0 = c_r0 + DV // NCOL
    c_end2 = c_g0 + 2 * D // NCOL
    ln_scope = main_scope.enter_context(ExitStack())
    ex = sb(ln_scope, "ex", [P, 3, TT, NCOL])
    e_pos, e_neg, e_rest = ex[:, 0], ex[:, 1], ex[:, 2]
    y_all = ex[:, 0:2].rearrange("p a t n -> p (a t n)").rearrange("p (c n) -> p c n", c=CT)
    xw = ex[:, 2].rearrange("p t n -> p (t n)")
    at = np.cumsum([0, NTOK, HIST + NP_TOK, STREAMS * (HIST + ST_TOK), NP_TOK, NTOK - NP_TOK, TAPS + 1]).tolist()
    u_in = xw[:, at[0]:at[1]].rearrange("p (t c) -> p t c", t=TT)
    full_p = xw[:, at[1]:at[2]]
    full_s = xw[:, at[2]:at[3]].rearrange("p (j n) -> p j n", j=STREAMS)
    sum_p = xw[:, at[3]:at[4]]
    sum_s = xw[:, at[4]:at[5]].rearrange("p (j n) -> p j n", j=STREAMS)
    taps = xw[:, at[5]:at[6]]
    with stage() as (st, block):
        lr_hi = sb(st, "lr_hi", [P, KD, RANK], F32R)
        lr_lo = sb(st, "lr_lo", [P, KD, RANK], F32R)
        zlr = sb(st, "zlr", [RANK + 1, NTOK])
        w_alpha = sb(st, "w_alpha_sb", [RANK + 1, NCOL])
        la = sb(st, "la", [P, TT, NCOL])
        decay = sb(st, "decay", [P, QK, 2 * TP + STREAMS])
        ob = sb(st, "ob", [P, TT, NCOL])
        sg = la
        lr_st = ob[:, 0, 0:KD * RANK].rearrange("p (k n) -> p k n", k=KD)
        s_lr, s_lrs, s_zlr, s_zcopy = sem("s_lr"), sem("s_lrs"), sem("s_zlr"), sem("s_zcopy")
        s_wal = sem("s_wal")
        m_ready = sem("m_ready")
        m_free = sem("m_free")
        s_soft, la_done = sem("s_soft"), sem("la_done")
        ob_free, kout_free = sem("ob_free"), sem("kout_free")
        s_ob = [sem(f"s_ob{t}") for t in range(TT)]
        s_kout, s_decay, decay_free, decay_ready = sem("s_kout"), sem("s_decay"), sem("decay_free"), sem("decay_ready")
        s_cin = sem("s_cin")
        s_ut, s_full = sem("s_ut"), sem("s_full")
        conv_done = sem("conv_done")
        outs_v = 2 * NHALF
        outs_u = outs_v + DV // NCOL
        outs_r = outs_u + CC // NCOL
        outs_g = outs_r + DV // NCOL
        NE = 2 * TT + 1
        NM = TT + NE

        def acc_before(c):
            return (c - NA) * TT + acc_base

        @block.sync
        def _(sp):
            sp.dma_start(lr_st, a["w_in"][:, C_LR:C_LR + RANK].rearrange("(k p) n -> p k n", p=P)).then_inc(s_lr, 16)
            with sp.Fori(0, NHALF) as i:
                sp.wait_ge(m_free, i * NE + 1)
                sp.dma_start(w_alpha[:], a["w_alpha"][:, bass.ds(i * NCOL, NCOL)]).then_inc(s_wal, 16)
                for q in range(QPC):
                    load_quarter(sp, i * 2 + c_q0, q, rows(a["w_in"], i * NCOL + C_Q, q))
                for q in range(QPC):
                    load_quarter(sp, i * 2 + (c_q0 + 1), q, rows(a["w_in"], i * NCOL + C_K, q))

            def load_chunks(c0, n, col):
                with sp.Fori(0, n) as i:
                    for q in range(QPC):
                        load_quarter(sp, i + c0, q, rows(a["w_in"], i * NCOL + col, q))

            load_chunks(c_v0, DV // NCOL, C_V)
            with sp.Fori(0, CC // NCOL) as i:
                for n, col in enumerate((C_G, C_A)):
                    for q in range(QPC):
                        load_quarter(sp, i * 2 + (c_u0 + n), q, rows(a["w_in"], i * NCOL + col, q))
            load_chunks(c_r0, DV // NCOL, C_R)
            load_chunks(c_g0, 2 * D // NCOL, C_GA)

        @block.gpsimd
        def _(pool):
            pool.sem_inc(ob_free, TT)
            pool.sem_inc(kout_free, TT)
            pool.sem_inc(decay_free, 1)

            def store(g, dst, col, outs):
                for t in range(TT):
                    pool.wait_ge(bank_free, g * TT + (TT + t + 1))
                    pool.sem_inc(store_gate, 1)
                    pool.dma_start(dst[t * P:(t + 1) * P, bass.ds(col, NCOL)], ob[:, t]).then_inc(s_ob[t], 16)

            def stored(outs):
                for t in range(TT):
                    pool.wait_ge(s_ob[t], outs * 16 + 16)
                    pool.sem_inc(ob_free, 1)

            def store_chunks(c0, n, dst, outs0):
                with pool.Fori(0, n) as i:
                    store(i + (c0 - NA), dst, i * NCOL, i + outs0)
                    stored(i + outs0)

            with pool.Fori(0, NHALF) as i:
                store(i * 2, d_qin, i * NCOL, i * 2)
                stored(i * 2)
                pool.wait_ge(decay_ready, i + 1)
                pool.sem_inc(store_gate, 1)
                pool.dma_start(d_decay[:, bass.ds(i * QK, QK), :], decay[:]).then_inc(s_decay, 16)
                store(i * 2 + 1, d_kin, i * NCOL, i * 2 + 1)
                for t in range(TT):
                    pool.dma_start(d_kout[t * P:(t + 1) * P, bass.ds(i * NCOL, NCOL)], e_pos[:, t]).then_inc(s_kout, 16)
                stored(i * 2 + 1)
                pool.wait_ge(s_kout, i * (16 * TT) + 16 * TT)
                pool.sem_inc(kout_free, TT)
                pool.wait_ge(s_decay, i * 16 + 16)
                pool.sem_inc(decay_free, 1)
            store_chunks(c_v0, DV // NCOL, d_v, outs_v)
            with pool.Fori(0, CC // NCOL) as i:
                store(i * 2 + (c_u0 - NA + 1), d_u, i * NCOL, i + outs_u)
                stored(i + outs_u)
            store_chunks(c_r0, DV // NCOL, d_r, outs_r)
            with pool.Fori(0, CT) as i:
                pool.wait_ge(conv_done, i + 1)
                pool.sem_inc(store_gate, 1)
                pool.dma_start(u_in, d_u[:, bass.ds(i * P, P)].rearrange("(t p) c -> p t c", p=P)).then_inc(s_cin, 16)
                pool.dma_start(full_s[:, :, 0:HIST], a["cacheT"][bass.ds(i * P, P), :, :]).then_inc(s_cin, 16)
                pool.dma_start(taps, a["taps"][bass.ds(i * P, P), :]).then_inc(s_cin, 16)
                store(i + (c_g0 - NA), d_gates, i * NCOL, i + outs_g)
                stored(i + outs_g)

        def small_bank(n):
            return ps[:, 5 + n % 3]

        AFTER = [range(0, 3), range(3, 7), range(7, 11), range(11, NM)]

        @block.tensor
        def _(pe):
            pe.wait_ge(s_lrs, 2)
            for k in range(KD):
                for n0, n1, bank in ((0, NP_TOK, 5), (NP_TOK, NTOK, 6)):
                    mm = product(pe, ps[0:RANK, bank, 0:n1 - n0], (lr_hi[:, k], lr_lo[:, k]),
                                 (act_hi[:, k, n0:n1], act_lo[:, k, n0:n1]), k == 0, k == KD - 1)
            mm.then_inc(s_zlr, 1)
            pe.wait_ge(s_zcopy, 3)

            def small(i, n):
                if n == 0:
                    pe.wait_ge(s_wal, i * 16 + 16)
                if 3 <= n < TT + 3:
                    pe.wait_ge(la_done, i * TT + (n - 2))
                else:
                    pe.wait_ge(m_free, i * NE + (1 if n < 3 else n - TT - 1))
                if n < TT:
                    mm = pe.matmul(small_bank(n), zlr[:, n * P:(n + 1) * P], w_alpha[:], start=True, stop=True)
                elif n < NM - 1:
                    t, rest = (n - TT) // 2, (n - TT) % 2
                    pe.wait_ge(la_done, i * TT + (t + 1))
                    at = (K_RESTP if rest else K_CUMP) if t < TP else (K_RESTS if rest else K_CUMS)
                    mm = pe.matmul(small_bank(n), kc[:, at:at + P], la[:, t], start=True, stop=True)
                else:
                    for j in range(QK):
                        for t in range(TT):
                            w, at = (2, K_INDP) if t < TP else (STREAMS, K_INDS)
                            c0 = j * (2 * TP + STREAMS) + 2 * t
                            mm = pe.matmul(small_bank(n)[:, c0:c0 + w], la[:, t, j * P:(j + 1) * P],
                                           kc[:, at:at + w], start=True, stop=True)
                mm.then_inc(m_ready, 1)

            with pe.Fori(0, NHALF) as i:
                def between(q):
                    for n in AFTER[q]:
                        small(i, n)

                multiply_chunk(pe, i * 2 + c_q0, i * 2, between=between)
                multiply_chunk(pe, i * 2 + (c_q0 + 1), i * 2 + 1)
            with pe.Fori(0, c_g0 - c_v0) as i:
                multiply_chunk(pe, i + c_v0, i + (c_v0 - NA))
            with pe.Fori(0, CT) as i:
                def turn_u(q):
                    if q == 0:
                        pe.wait_ge(s_cin, i * 48 + 48)
                        for t in range(TT):
                            mm = pe.transpose(ps[:, 5 + t // 4, t % 4 * P:t % 4 * P + P], u_in[:, t], ident)
                        mm.then_inc(s_ut, 1)

                multiply_chunk(pe, i + c_g0, i + (c_g0 - NA), between=turn_u)

        def take(act, g, outs, func, dst=None):
            for t in range(TT):
                act.wait_ge(acc_done, g * TT + (acc_base + t + 1))
                if dst is None:
                    act.wait_ge(ob_free, outs * TT + (t + 1))
                act.activation((ob if dst is None else dst)[:, t], ps[:, t], func).then_inc(bank_free, 1)

        @block.scalar
        def _(act):
            lk = link(act, "act")
            act.sem_inc(m_free, 1)
            act.wait_ge(s_lr, 16)
            act.activation(lr_hi[:], lr_st, ACT.Copy).then_inc(s_lrs, 1)
            act.wait_ge(s_zlr, 1)
            act.wait_ge(s_zcopy, 1)
            act.activation(zlr[0:RANK, 0:NP_TOK], ps[0:RANK, 5], ACT.Copy).then_inc(s_zcopy, 1)
            act.activation(zlr[0:RANK, NP_TOK:NTOK], ps[0:RANK, 6, 0:NTOK - NP_TOK], ACT.Copy).then_inc(s_zcopy, 1)

            def small(i, n):
                act.wait_ge(m_ready, i * NM + (n + 1))
                src = small_bank(n)
                if n < TT:
                    s = la[:, n]
                    lk.mark(act.activation(s, src, ACT.Abs))
                    lk.sync()
                    lk.mark(act.activation(s, s, ACT.Exp, scale=-1.0))
                    lk.sync()
                    act.activation(s, s, ACT.Ln, bias=1.0).then_inc(s_soft, 1)
                elif n < NM - 1:
                    t, rest = (n - TT) // 2, (n - TT) % 2
                    if rest:
                        act.activation(e_rest[:, t], src, ACT.Exp, scale=1.0 / GATE_NORM).then_inc(m_free, 1)
                    else:
                        act.wait_ge(kout_free, i * TT + TT)
                        lk.mark(act.activation(e_pos[:, t], src, ACT.Exp, scale=1.0 / GATE_NORM))
                        act.activation(e_neg[:, t], src, ACT.Exp, scale=-1.0 / GATE_NORM).then_inc(m_free, 1)
                else:
                    act.wait_ge(decay_free, i + 1)
                    lk.mark(act.activation(decay[:].rearrange("p j n -> p (j n)"),
                                           src[:, 0:QK * (2 * TP + STREAMS)], ACT.Exp, scale=1.0 / GATE_NORM))
                    lk.sync()
                    act.sem_inc(decay_ready, 1)
                    act.sem_inc(m_free, 1)

            split_hi(act, c_q0, 0, acc_base)
            with act.Fori(0, NHALF) as i:
                lk.enter(i, 2 * TT + TT + 1)
                for q in range(1, QPC + 1):
                    split_hi(act, i * 2 + (c_q0 + q // QPC), q % QPC, i * (2 * TT) + acc_base)
                    for n in AFTER[q - 1]:
                        small(i, n)
                for q in range(1, QPC + 1):
                    split_hi(act, i * 2 + (c_q0 + 1 + q // QPC), q % QPC, i * (2 * TT) + (acc_base + TT))
                lk.leave_step()
            lk.leave(NHALF)

            def splits(c, g):
                for q in range(1, QPC):
                    split_hi(act, c, q, g * TT + acc_base)
                split_hi(act, c + 1, 0, acc_base)

            def take_chunks(c0, n, func, outs0):
                with act.Fori(0, n) as i:
                    splits(i + c0, i + (c0 - NA))
                    take(act, i + (c0 - NA), i + outs0, func)

            take_chunks(c_v0, DV // NCOL, ACT.Copy, outs_v)
            with act.Fori(0, CC // NCOL) as i:
                g = i * 2 + (c_u0 - NA)
                splits(i * 2 + c_u0, g)
                act.wait_ge(bank_free, g * TT + TT)
                take(act, g, 0, ACT.Sigmoid, sg)
                splits(i * 2 + (c_u0 + 1), g + 1)
            take_chunks(c_r0, DV // NCOL, ACT.Silu, outs_r)

            def gates_and_u(i, last):
                g = i + (c_g0 - NA)
                for q in (1, 2):
                    split_hi(act, i + c_g0, q, g * TT + acc_base)
                act.wait_ge(s_ut, i + 1)
                act.activation(full_p[:, HIST:HIST + NP_TOK], ps[:, 5], ACT.Copy)
                act.activation(full_s[:, :, HIST:HIST + ST_TOK],
                               ps[:, 6, 0:P].rearrange("p (j n) -> p j n", j=STREAMS), ACT.Copy).then_inc(s_full, 1)
                split_hi(act, i + c_g0, 3, g * TT + acc_base)
                if not last:
                    split_hi(act, i + (c_g0 + 1), 0, acc_base)
                take(act, g, i + outs_g, ACT.Sigmoid)

            with act.Fori(0, CT - 1) as i:
                gates_and_u(i, False)
            gates_and_u(CT - 1, True)

        @block.vector
        def _(dve):
            lk = link(dve, "dve")
            dve.memset(zlr[:], 1.0).then_inc(s_zcopy, 1)
            dve.wait_ge(s_lrs, 1)
            dve.tensor_tensor(lr_lo[:], lr_st, lr_hi[:].bitcast(F32), ALU.subtract).then_inc(s_lrs, 1)

            def small(i, n):
                if n < TT:
                    dve.wait_ge(s_soft, i * TT + (n + 1))
                    dve.scalar_tensor_tensor(out=la[:, n], in0=small_bank(n), scalar=0.0, in1=la[:, n],
                                             op0=ALU.min, op1=ALU.subtract).then_inc(la_done, 1)

            def splits(c):
                for q in range(1, QPC):
                    split_lo(dve, c, q)
                split_lo(dve, c + 1, 0)

            split_lo(dve, c_q0, 0)
            with dve.Fori(0, NHALF) as i:
                lk.enter(i, TT)
                for q in range(1, QPC + 1):
                    split_lo(dve, i * 2 + (c_q0 + q // QPC), q % QPC)
                    for n in AFTER[q - 1]:
                        small(i, n)
                dve.wait_ge(m_free, i * NE + (NE + 1))
                for t in range(TT):
                    dve.wait_ge(acc_done, i * (2 * TT) + (acc_base + t + 1))
                    dve.wait_ge(ob_free, i * (2 * TT) + (t + 1))
                    dve.scalar_tensor_tensor(out=ob[:, t], in0=ps[:, t], scalar=DKH ** -0.5, in1=e_pos[:, t],
                                             op0=ALU.mult, op1=ALU.mult).then_inc(bank_free, 1)
                splits(i * 2 + (c_q0 + 1))
                for t in range(TT):
                    dve.wait_ge(acc_done, i * (2 * TT) + (acc_base + TT + t + 1))
                    dve.wait_ge(ob_free, i * (2 * TT) + (TT + t + 1))
                    lk.mark(dve.tensor_tensor(ob[:, t], ps[:, t], e_neg[:, t], ALU.mult))
                    dve.tensor_tensor(e_pos[:, t], ps[:, t], e_rest[:, t], ALU.mult).then_inc(bank_free, 1)
                lk.leave_step()
            lk.leave(NHALF)
            with dve.Fori(0, DV // NCOL) as i:
                splits(i + c_v0)
            with dve.Fori(0, CC // NCOL) as i:
                g = i * 2 + (c_u0 - NA)
                splits(i * 2 + c_u0)
                splits(i * 2 + (c_u0 + 1))
                for t in range(TT):
                    dve.wait_ge(acc_done, (g + 1) * TT + (acc_base + t + 1))
                    dve.wait_ge(ob_free, (i + outs_u) * TT + (t + 1))
                    dve.tensor_tensor(ob[:, t], ps[:, t], sg[:, t], ALU.mult).then_inc(bank_free, 1)
            with dve.Fori(0, c_g0 - c_r0) as i:
                splits(i + c_r0)
            dve.sem_inc(conv_done, 1)
            lk.mark(dve.memset(full_p[:, 0:HIST], 0.0))
            dve.wait_ge(kout_free, (NHALF + 1) * TT)

            def convolve(i, k0, k1):
                for k in range(k0, k1):
                    p, s, w = full_p[:, k:k + NP_TOK], full_s[:, :, k:k + ST_TOK], taps[:, k:k + 1]
                    out_p, out_s = sum_p, sum_s
                    if k == TAPS - 1:
                        y = y_all[:, bass.ds(i, 1)].rearrange("p o n -> p (o n)")
                        out_p = y[:, 0:NP_TOK]
                        out_s = y[:, NP_TOK:NTOK].rearrange("p (j n) -> p j n", j=STREAMS)
                    for src, total, out in ((p, sum_p, out_p), (s, sum_s, out_s)):
                        if k == 0:
                            lk.sync()
                            ins = dve.tensor_scalar(out, src, w, taps[:, TAPS:TAPS + 1], ALU.mult, ALU.add)
                        else:
                            lk.sync(back=1)
                            ins = dve.scalar_tensor_tensor(out=out, in0=src, scalar=w, in1=total,
                                                           op0=ALU.mult, op1=ALU.add)
                        lk.mark(ins)

            def step(i, last):
                split_lo(dve, i + c_g0, 1)
                split_lo(dve, i + c_g0, 2)
                dve.wait_ge(s_full, i + 1)
                convolve(i, 0, TAPS // 2)
                split_lo(dve, i + c_g0, 3)
                convolve(i, TAPS // 2, TAPS)
                lk.sync()
                dve.sem_inc(conv_done, 1)
                if not last:
                    split_lo(dve, i + (c_g0 + 1), 0)

            with dve.Fori(0, CT - 1) as i:
                lk.enter(i, 2 * TAPS)
                step(i, False)
                lk.leave_step()
            lk.leave(CT - 1)
            step(CT - 1, True)


    c_cv0 = c_end2
    g_cv0 = c_end2 - NA
    N_CV = D // NCOL // 2
    with stage() as (st, block):
        lnp = sb(st, "lnp_sb", [P, 2, CT])
        gt = sb(st, "gt", [P, TT, NCOL])
        ob = sb(st, "ob4", [P, TT, NCOL])
        mean, rstd = xw[:, 0:NTOK], xw[:, NTOK:2 * NTOK]
        sq = xw[:, 2 * NTOK:4 * NTOK].rearrange("p (a n) -> p a n", a=2)
        s_lnp, s_sum, s_mean, s_cent, s_sq, s_var = (sem("c4_" + n) for n in ("lnp", "sum", "mean", "cent", "sq", "var"))
        s_std, s_norm, s_silu, s_yhi, s_ylo, s_vs = (sem("c4_" + n) for n in ("std", "norm", "silu", "yhi", "ylo", "vs"))
        ob_free, s_gate = sem("c4_obfree"), sem("c4_gate")
        s_ob = [sem(f"c4_ob{t}") for t in range(TT)]
        s_cache = sem("s_cache")

        @block.sync
        def _(sp):
            sp.dma_start(lnp[:], a["lnp"]).then_inc(s_lnp, 16)
            with sp.Fori(0, N_CV) as i:
                for q in range(QPC):
                    load_quarter(sp, i + c_cv0, q, rows(a["w_conv_o"], i * (2 * NCOL) + q // 2 * NCOL, q % 2))

        @block.gpsimd
        def _(pool):
            pool.sem_inc(ob_free, TT)
            pool.dma_start(a["out_cp"], d_u[NP_TOK - HIST:NP_TOK, :]).then_inc(s_cache, 16)
            pool.dma_start(a["out_cs"][:, 0:HIST - ST_TOK, :], a["cache"][:, ST_TOK:HIST, :]).then_inc(s_cache, 16)
            pool.dma_start(a["out_cs"][:, HIST - ST_TOK:HIST, :],
                           d_u[NP_TOK:NTOK, :].rearrange("(j n) c -> j n c", j=STREAMS)).then_inc(s_cache, 16)
            with pool.Fori(0, 2 * N_CV) as i:
                for t in range(TT):
                    pool.wait_ge(bank_free, (i + g_cv0) * TT + (TT + t + 1))
                    pool.sem_inc(store_gate, 1)
                    pool.dma_start(d_mb[t * P:(t + 1) * P, bass.ds(i * NCOL, NCOL)], ob[:, t]).then_inc(s_ob[t], 16)
                for t in range(TT):
                    pool.wait_ge(s_ob[t], i * 16 + 16)
                    pool.sem_inc(ob_free, 1)
            pool.wait_ge(s_cache, 48)

        @block.tensor
        def _(pe):
            for part, ready in enumerate((None, s_sq)):
                for k in range(CT):
                    if ready is not None:
                        pe.wait_ge(ready, k + 1)
                    src = y_all[:, k] if part == 0 else sq[:, k % 2]
                    for n0, n1, bank in ((0, NP_TOK, 5 - part * 4), (NP_TOK, NTOK, 6 - part * 4)):
                        mm = pe.matmul(ps[:, bank, 0:n1 - n0], kc[:, K_ONES:K_ONES + P], src[:, n0:n1],
                                       start=k == 0, stop=k == CT - 1)
                    if part == 1 or k == CT - 1:
                        mm.then_inc((s_sum, s_var)[part], 1)
            pe.wait_ge(s_ylo, CT)
            with pe.Fori(0, N_CV) as i:
                for n in range(2):
                    multiply_chunk(pe, i + c_cv0, i * 2 + (g_cv0 + n), quarters=2, q0=2 * n)
                    if n == 0:
                        pe.wait_ge(w_used, i * (QPC - 1) + (c_cv0 * (QPC - 1) + 2))
                        pe.sem_inc(w_used, 1)

        @block.scalar
        def _(act):
            lk = link(act, "act")
            act.wait_ge(s_lnp, 16)
            for k in range(CT):
                act.wait_ge(s_cent, k + 1)
                if k > 1:
                    act.wait_ge(s_var, k - 1)
                act.activation(sq[:, k % 2], y_all[:, k], ACT.Square).then_inc(s_sq, 1)
            act.wait_ge(s_vs, 1)
            act.activation(rstd, rstd, ACT.Sqrt).then_inc(s_std, 1)
            split_hi(act, c_cv0, 0, acc_base)
            for k in range(CT):
                act.wait_ge(s_norm, k + 1)
                act.activation(y_all[:, k], y_all[:, k], ACT.Silu, scale=lnp[:, 0, k:k + 1],
                               bias=lnp[:, 1, k:k + 1]).then_inc(s_silu, 1)
                act.wait_ge(s_silu, k + 1)
                act.activation(act_hi[:, k, :], y_all[:, k], ACT.Copy).then_inc(s_yhi, 1)

            def gates(i, n):
                g = i * 2 + (g_cv0 + n)
                act.wait_ge(bank_free, g * TT + TT)
                for t in range(TT):
                    act.dma_start(gt[:, t], d_gates[t * P:(t + 1) * P, bass.ds(i * (2 * NCOL) + (D + n * NCOL), NCOL)]
                                  ).then_inc(s_gate, 16)

            def step(i, last):
                c, before = i + c_cv0, (i * 2 + g_cv0) * TT + acc_base
                split_hi(act, c, 1, before)
                gates(i, 0)
                split_hi(act, c, 2, before)
                act.wait_ge(acc_done, before + TT)
                split_hi(act, c, 3, before)
                gates(i, 1)
                if not last:
                    split_hi(act, c + 1, 0, before)

            for i in range(N_CV):
                step(i, i == N_CV - 1)

        @block.vector
        def _(dve):
            lk = link(dve, "dve")
            dve.wait_ge(s_sum, 1)
            for n0, n1, bank in ((0, NP_TOK, 5), (NP_TOK, NTOK, 6)):
                lk.mark(dve.tensor_scalar(mean[:, n0:n1], ps[:, bank, 0:n1 - n0], 1.0 / CC, None, ALU.mult))
            lk.sync()
            for k in range(CT):
                dve.tensor_tensor(y_all[:, k], y_all[:, k], mean, ALU.subtract).then_inc(s_cent, 1)
            dve.wait_ge(s_var, CT)
            for n0, n1, bank in ((0, NP_TOK, 1), (NP_TOK, NTOK, 2)):
                lk.mark(dve.tensor_scalar(rstd[:, n0:n1], ps[:, bank, 0:n1 - n0], 1.0 / CC, EPS, ALU.mult, ALU.add))
            lk.sync()
            dve.sem_inc(s_vs, 1)
            dve.wait_ge(s_std, 1)
            lk.mark(dve.reciprocal(rstd, rstd))
            lk.sync()
            split_lo(dve, c_cv0, 0)
            dve.wait_ge(s_cent, CT)
            for k in range(CT):
                dve.tensor_tensor(y_all[:, k], y_all[:, k], rstd, ALU.mult).then_inc(s_norm, 1)
            for k in range(CT):
                dve.wait_ge(s_yhi, k + 1)
                dve.tensor_tensor(act_lo[:, k, :], y_all[:, k], act_hi[:, k, :].bitcast(F32),
                                  ALU.subtract).then_inc(s_ylo, 1)

            def take(i, n):
                g = i * 2 + (g_cv0 + n)
                dve.wait_ge(s_gate, i * (32 * TT) + (n + 1) * 16 * TT)
                for t in range(TT):
                    dve.wait_ge(acc_done, g * TT + (acc_base + t + 1))
                    dve.wait_ge(ob_free, (i * 2 + n) * TT + (t + 1))
                    dve.tensor_tensor(ob[:, t], ps[:, t], gt[:, t], ALU.mult).then_inc(bank_free, 1)

            for i in range(N_CV):
                split_lo(dve, i + c_cv0, 1)
                split_lo(dve, i + c_cv0, 2)
                take(i, 0)
                split_lo(dve, i + c_cv0, 3)
                if i < N_CV - 1:
                    split_lo(dve, i + c_cv0 + 1, 0)
                take(i, 1)
    ln_scope.close()

    NCI = 2 * TP
    NU = NCI + STREAMS
    with stage() as (st, block):
        NS = 3
        qk = sb(st, "qk", [P, NS, 3, DKH])
        vt = sb(st, "vt", [P, NS, DVH])
        rt = sb(st, "rt", [P, NS, DVH])
        q_diag = sb(st, "q_diag", [P, 2, 2, 2 * P])
        q_diag_s = sb(st, "q_diag_s", [P, 2, STREAMS * P])
        k_t = sb(st, "k_t", [P, NS, 2, P])
        att = sb(st, "att", [P, NS, P])
        k_rows = sb(st, "k_rows", [P, 4, DKH])
        state = sb(st, "state_sb", [P, 2, 2, DVH])
        dec = sb(st, "dec", [P, 2, NU])
        g_out = sb(st, "g_out", [P, DVH])
        sq = sb(st, "sq", [P, DVH])
        ss = sb(st, "ss3", [P, TT, 4])
        o_sb = sb(st, "o_sb", [P, NS, DVH])
        s0 = w_in_st[:].rearrange("p a b n -> p (a b) n")

        s_in = [sem(f"s_in{t}") for t in range(TT)]
        s_gout, s_dec, s_s0 = sem("s_gout"), sem("s_dec"), sem("s_s0")
        s_zero = sem("s_zero")
        tile_pe = sem("tile_pe")
        post_done = sem("post_done")
        tr_ready, tr_taken = sem("tr_ready"), sem("tr_taken")
        at_ready, at_taken = sem("at_ready"), sem("at_taken")
        ds_ready = sem("ds_ready")
        ds_taken = sem("ds_taken")
        k_ready, r_ready, o_ready = sem("k_ready"), sem("r_ready"), sem("o_ready")
        s_sq, s_ms, s_sd = sem("s_sq"), sem("s_ms"), sem("s_sd")
        o_free = sem("o_free")
        state_free = sem("state_free")
        s0_free = sem("s0_free")
        s_o = [sem(f"s_o{n}") for n in range(NS)]
        s_sp, s_st = sem("s_sp"), sem("s_st")

        @block.sync
        def _(sp):
            sp.dma_start(g_out[:], a["g_gla_out"].broadcast_to([P, DVH])).then_inc(s_gout, 16)
            with sp.Fori(0, HEADS) as h:
                for t in range(TT):
                    seen = h * TT + (t + 1 if t >= NS else (2, 3, 1)[t])
                    sp.wait_ge(tile_pe, seen)
                    sp.wait_ge(post_done, seen)
                    rows_t = slice(t * P, (t + 1) * P)
                    for n, src in enumerate((d_qin, d_kin, d_kout)):
                        sp.dma_start(qk[:, t % NS, n], src[rows_t, bass.ds(h * DKH, DKH)]).then_inc(s_in[t], 16)
                    sp.dma_start(vt[:, t % NS], d_v[rows_t, bass.ds(h * DVH, DVH)]).then_inc(s_in[t], 16)
                    sp.dma_start(rt[:, t % NS], d_r[rows_t, bass.ds(h * DVH, DVH)]).then_inc(s_in[t], 16)
                    if t == 0:
                        sp.wait_ge(ds_taken, h * NU + 4)
                        sp.dma_start(dec[:], d_decay[:, bass.ds(h * 2, 2), :]).then_inc(s_dec, 16)
                    if t == 2:
                        sp.wait_ge(s0_free, h + 1)
                        for j in range(STREAMS):
                            sp.dma_start(s0[:, 2 * j:2 * j + 2, :],
                                         a["state"][j, bass.ds(h * DKH, DKH), :].rearrange("(k p) n -> p k n", p=P)
                                         ).then_inc(s_s0, 16)

        @block.gpsimd
        def _(pool):
            pool.sem_inc(o_free, 2)
            pool.sem_inc(state_free, 1)
            pool.sem_inc(s0_free, 1)
            pool.wait_ge(s_gout, 16)

            def stored(h, t):
                pool.wait_ge(s_o[t % NS], h * (32 if t % NS < 2 else 16) + (32 if t >= NS else 16))
                pool.sem_inc(o_free, 1)

            def store_o(h, t):
                pool.wait_ge(post_done, h * TT + (t + 4))
                pool.sem_inc(store_gate, 1)
                pool.dma_start(d_o[t * P:(t + 1) * P, bass.ds(h * DVH, DVH)], o_sb[:, t % NS]).then_inc(s_o[t % NS], 16)

            def mask_rows(h, t, n):
                u = 2 * t + n
                at = (K_INDP if t < TP else K_INDS) + n
                pool.wait_ge(ds_taken, h * NU + (u + 1))
                pool.sem_inc(store_gate, 1)
                pool.tensor_scalar(k_rows[:, u % 4], qk[:, t % NS, 2], kc[:, at:at + 1], None,
                                   ALU.mult).then_inc(k_ready, 1)

            with pool.Fori(0, HEADS) as h:
                for t in range(TT):
                    pool.wait_ge(s_in[t], h * 80 + 80)
                    pool.tensor_tensor(rt[:, t % NS], rt[:, t % NS], g_out[:], ALU.mult).then_inc(r_ready, 1)
                    for n in range(2 if t < TP else 4):
                        mask_rows(h, t, n)
                    if t > 0:
                        store_o(h, t - 1)
                        if t > 1:
                            stored(h, t - 2)
                    if t == TP:
                        pool.wait_ge(ds_taken, h * NU + (NCI + 4))
                        pool.sem_inc(store_gate, 1)
                        pool.dma_start(a["out_sp"][bass.ds(h * DKH, DKH), :].rearrange("(k p) n -> p k n", p=P),
                                       state[:, NCI % 2]).then_inc(s_sp, 16)
                for n in range(4, STREAMS):
                    mask_rows(h, TP, n)
                store_o(h, TT - 1)
                for j in range(STREAMS):
                    pool.wait_ge(ds_taken, h * NU + (NCI + j + 5))
                    pool.sem_inc(store_gate, 1)
                    pool.dma_start(a["out_ss"][j, bass.ds(h * DKH, DKH), :].rearrange("(k p) n -> p k n", p=P),
                                   s0[:, 2 * j:2 * j + 2, :]).then_inc(s_st, 16)
                stored(h, TT - 2)
                stored(h, TT - 1)
                pool.wait_ge(s_sp, h * 16 + 16)
                pool.sem_inc(state_free, 1)
                pool.wait_ge(s_st, h * (16 * STREAMS) + 16 * STREAMS)
                pool.sem_inc(s0_free, 1)

        def diag(t, k):
            if t < TP:
                return q_diag[:, t % 2, k].rearrange("p (a b) -> p a b", b=CHUNK)[:, 0:4:3, :]
            return q_diag_s[:, k].rearrange("p (a b) -> p a b", b=ST_TOK)[:, 0:9 * STREAMS - 8:9, :]

        @block.tensor
        def _(pe):
            pe.sem_inc(tile_pe, 3)
            pe.wait_ge(s_zero, 2)

            def turn(h, t):
                pe.wait_ge(s_in[t], h * 80 + 80)
                pe.wait_ge(tr_taken, h * TT + (t + 1))
                for n in range(2):
                    for k in range(2):
                        c0 = (2 * n + k) * P
                        mm = pe.transpose(ps[:, 0, c0:c0 + P], qk[:, t % NS, n, k * P:(k + 1) * P], ident)
                mm.then_inc(tr_ready, 1)

            def update(h, u, slot):
                pe.wait_ge(k_ready, h * NU + (u + 1))
                pe.wait_ge(ds_taken, h * NU + (u + 3))
                for k in range(2):
                    mm = pe.matmul(ps[:, 4 + 2 * (u % 2) + k], k_rows[:, u % 4, k * P:(k + 1) * P], vt[:, slot],
                                   start=True, stop=True)
                mm.then_inc(ds_ready, 1)

            with pe.Fori(0, HEADS) as h:
                turn(h, 0)
                for t in range(TT):
                    slot, o = t % NS, ps[:, 2 + t % 2]
                    pe.wait_ge(tr_taken, h * TT + (t + 2))
                    for k in range(2):
                        mm = pe.matmul(ps[:, 1, 0:P], k_t[:, slot, k], diag(t, k), start=k == 0, stop=k == 1)
                    mm.then_inc(at_ready, 1)
                    pe.wait_ge(post_done, h * TT + (t + (3 if t == 0 else 2)))
                    first = True
                    if t == TP:
                        pe.wait_ge(s_s0, h * (16 * STREAMS) + 16 * STREAMS)
                        for j in range(STREAMS):
                            for k in range(2):
                                pe.matmul(o, q_diag_s[:, k, j * P:(j + 1) * P], s0[:, 2 * j + k], start=first,
                                          stop=False)
                                first = False
                    elif t > 0:
                        pe.wait_ge(ds_taken, h * NU + (2 * t + 4))
                        for k in range(2):
                            pe.matmul(o, q_diag[:, t % 2, k, 0:P], state[:, 0, k], start=first, stop=False)
                            first = False
                    if t < TT - 1:
                        turn(h, t + 1)
                    pe.wait_ge(at_taken, h * TT + (t + 1))
                    mm = pe.matmul(o, att[:, slot], vt[:, slot], start=first, stop=t == TP)
                    if t == TP:
                        mm.then_inc(o_ready, 1)
                        for j in range(STREAMS):
                            update(h, NCI + j, slot)
                    else:
                        update(h, 2 * t, slot)
                        update(h, 2 * t + 1, slot)
                        pe.wait_ge(ds_taken, h * NU + (2 * t + 5))
                        for k in range(2):
                            mm = pe.matmul(o, q_diag[:, t % 2, k, P:2 * P], state[:, 1, k], start=False,
                                           stop=k == 1)
                        mm.then_inc(o_ready, 1)
                    pe.wait_ge(o_ready, h * TT + (t + 1))
                    pe.wait_ge(ds_ready, h * NU + (2 * t + 2 if t < TP else NU))
                    pe.sem_inc(tile_pe, 1)

        @block.scalar
        def _(act):
            lk = link(act, "act")
            act.sem_inc(tr_taken, 1)

            def take_turned(h, t):
                act.wait_ge(tr_ready, h * TT + (t + 1))
                act.wait_ge(tile_pe, h * TT + (t + 2))
                for k in range(2):
                    w = CHUNK if t < TP else ST_TOK
                    lk.mark(act.activation(diag(t, k), ps[:, 0, k * P:(k + 1) * P].rearrange("p (c b) -> p c b", b=w),
                                           ACT.Copy))
                act.activation(k_t[:, t % NS].rearrange("p k n -> p (k n)"), ps[:, 0, 2 * P:4 * P],
                               ACT.Copy).then_inc(tr_taken, 1)

            with act.Fori(0, HEADS) as h:
                lk.enter(h, 2 * TT + TT)
                take_turned(h, 0)
                for t in range(TT):
                    if t < TT - 1:
                        take_turned(h, t + 1)
                    act.wait_ge(o_ready, h * TT + (t + 1))
                    lk.sync()
                    lk.mark(act.activation(sq[:], ps[:, 2 + t % 2], ACT.Square, accum_out=ss[:, t, 0:1]))
                    lk.sync()
                    act.sem_inc(s_sq, 1)
                    act.wait_ge(s_ms, h * TT + (t + 1))
                    act.activation(ss[:, t, 2:3], ss[:, t, 1:2], ACT.Sqrt).then_inc(s_sd, 1)
                lk.leave_step()
            lk.leave(HEADS)

        @block.vector
        def _(dve):
            lk = link(dve, "dve")
            dve.sem_inc(post_done, 3)
            dve.sem_inc(ds_taken, 4)
            dve.memset(q_diag[:], 0.0).then_inc(s_zero, 1)
            dve.memset(q_diag_s[:], 0.0).then_inc(s_zero, 1)

            def update(h, u):
                dve.wait_ge(ds_ready, h * NU + (u + 1))
                if u == 1:
                    dve.wait_ge(state_free, h + 1)
                for k in range(2):
                    got = ps[:, 4 + 2 * (u % 2) + k]
                    if u >= NCI:
                        old = new = s0[:, 2 * (u - NCI) + k]
                    else:
                        old, new = state[:, u % 2, k], state[:, (u + 1) % 2, k]
                    if u == 0:
                        ins = dve.tensor_copy(new, got)
                    else:
                        ins = dve.scalar_tensor_tensor(out=new, in0=old, scalar=dec[:, k, u:u + 1], in1=got,
                                                       op0=ALU.mult, op1=ALU.add)
                    if k == 0:
                        lk.mark(ins)
                    else:
                        ins.then_inc(ds_taken, 1)

            with dve.Fori(0, HEADS) as h:
                lk.enter(h, NU + TT)
                dve.wait_ge(s_dec, h * 16 + 16)
                for t in range(TT):
                    dve.wait_ge(at_ready, h * TT + (t + 1))
                    at = K_CUMP if t < TP else K_CUMS
                    dve.tensor_tensor(att[:, t % NS], ps[:, 1, 0:P], kc[:, at:at + P], ALU.mult).then_inc(at_taken, 1)
                    if t < TP:
                        update(h, 2 * t)
                        dve.wait_ge(ds_taken, h * NU + (2 * t + 5))
                        update(h, 2 * t + 1)
                    dve.wait_ge(s_sq, h * TT + (t + 1))
                    dve.tensor_scalar(ss[:, t, 1:2], ss[:, t, 0:1], 1.0 / DVH, EPS, ALU.mult, ALU.add).then_inc(s_ms, 1)
                    dve.wait_ge(s_sd, h * TT + (t + 1))
                    lk.mark(dve.reciprocal(ss[:, t, 3:4], ss[:, t, 2:3]))
                    lk.sync()
                    dve.wait_ge(r_ready, h * TT + (t + 1))
                    dve.wait_ge(o_free, h * TT + (t + 1))
                    dve.scalar_tensor_tensor(out=o_sb[:, t % NS], in0=ps[:, 2 + t % 2], scalar=ss[:, t, 3:4],
                                             in1=rt[:, t % NS], op0=ALU.mult, op1=ALU.mult).then_inc(post_done, 1)
                    if t == TP:
                        for j in range(STREAMS):
                            update(h, NCI + j)
                lk.leave_step()
            lk.leave(HEADS)

    def project_stage(name, weight, dst, c0, g0, src=None, G0=0, gated=False):
        n_ch = D // NCOL
        with stage() as (st, block):
            xt = sb(st, name + "_x", [P, 4, NCOL])
            ob = sb(st, name + "_ob", [P, TT, NCOL])
            s_x = [sem(f"{name}_x{g}") for g in range(4)]
            ob_free, s_gate = sem(name + "_obfree"), sem(name + "_gate")
            s_ob = [sem(f"{name}_ob{t}") for t in range(TT)]
            if gated:
                gt = sb(st, name + "_gt", [P, TT, NCOL])
                mt = sb(st, name + "_mt", [P, TT, NCOL])

            @block.sync
            def _(sp):
                for q in range(QPC):
                    load_quarter(sp, c0, q, rows(weight, 0, q))
                if src is not None:
                    with sp.Fori(0, TT) as t:
                        for g in range(4):
                            sp.wait_ge(t_taken, t * 4 + (G0 + g + 1))
                            sp.dma_start(xt[:, g], src[bass.ds(t * P, P), g * NCOL:(g + 1) * NCOL]).then_inc(s_x[g], 16)
                with sp.Fori(1, n_ch) as i:
                    for q in range(QPC):
                        load_quarter(sp, i + c0, q, rows(weight, i * NCOL, q))

            @block.gpsimd
            def _(pool):
                pool.sem_inc(ob_free, TT)
                with pool.Fori(0, n_ch) as i:
                    for t in range(TT):
                        pool.wait_ge(bank_free, (i + g0) * TT + (TT + t + 1))
                        pool.sem_inc(store_gate, 1)
                        pool.dma_start(dst[t * P:(t + 1) * P, bass.ds(i * NCOL, NCOL)], ob[:, t]).then_inc(s_ob[t], 16)
                    for t in range(TT):
                        pool.wait_ge(s_ob[t], i * 16 + 16)
                        pool.sem_inc(ob_free, 1)

            @block.tensor
            def _(pe):
                if src is not None:
                    with pe.Fori(0, TT) as t:
                        for g in range(4):
                            pe.wait_ge(s_x[g], t * 16 + 16)
                            transpose_group(pe, t * 4 + (G0 + g), g, xt[:, g])
                    pe.wait_ge(t_taken, G0 + 4 * TT + 4)
                with pe.Fori(0, n_ch) as i:
                    multiply_chunk(pe, i + c0, i + g0)

            @block.scalar
            def _(act):
                split_hi(act, c0, 0, acc_base)
                if src is not None:
                    with act.Fori(0, TT) as t:
                        for g in range(4):
                            take_hi(act, t * 4 + (G0 + g), g, t)

                def step(i, last):
                    for q in range(1, QPC):
                        split_hi(act, i + c0, q, (i + g0) * TT + acc_base)
                        if q == 1 and gated:
                            act.wait_ge(bank_free, (i + g0) * TT + TT)
                            for t in range(TT):
                                tile = (slice(t * P, (t + 1) * P), bass.ds(i * NCOL, NCOL))
                                act.dma_start(gt[:, t], d_gates[tile]).then_inc(s_gate, 16)
                                act.dma_start(mt[:, t], d_mb[tile]).then_inc(s_gate, 16)
                    if not last:
                        split_hi(act, i + (c0 + 1), 0, acc_base)
                    if not gated:
                        for t in range(TT):
                            act.wait_ge(acc_done, (i + g0) * TT + (acc_base + t + 1))
                            act.wait_ge(ob_free, i * TT + (t + 1))
                            act.activation(ob[:, t], ps[:, t], ACT.Copy).then_inc(bank_free, 1)

                with act.Fori(0, n_ch - 1) as i:
                    step(i, False)
                step(n_ch - 1, True)

            @block.vector
            def _(dve):
                lk = link(dve, "dve")
                split_lo(dve, c0, 0)
                if src is not None:
                    with dve.Fori(0, TT) as t:
                        for g in range(4):
                            take_lo(dve, t * 4 + (G0 + g), g, t)

                def step(i, last):
                    for q in range(1, QPC):
                        split_lo(dve, i + c0, q)
                    if not last:
                        split_lo(dve, i + (c0 + 1), 0)
                    if gated:
                        dve.wait_ge(s_gate, i * (32 * TT) + 32 * TT)
                        for t in range(TT):
                            dve.wait_ge(acc_done, (i + g0) * TT + (acc_base + t + 1))
                            dve.wait_ge(ob_free, i * TT + (t + 1))
                            lk.mark(dve.tensor_tensor(ob[:, t], ps[:, t], gt[:, t], ALU.mult))
                            lk.sync()
                            dve.tensor_tensor(ob[:, t], ob[:, t], mt[:, t], ALU.add).then_inc(bank_free, 1)

                with dve.Fori(0, n_ch - 1) as i:
                    if gated:
                        lk.enter(i, TT)
                    step(i, False)
                    if gated:
                        lk.leave_step()
                if gated:
                    lk.leave(n_ch - 1)
                step(n_ch - 1, True)

    n_ch = D // NCOL
    c_o0, g_o0 = c_cv0 + N_CV, g_cv0 + 2 * N_CV
    project_stage("yo", a["w_gla_o"], d_m, c_o0, g_o0, src=d_o, G0=t_groups, gated=True)
    t_groups += 4 * TT
    project_stage("mo", a["w_out"], d_mix, c_o0 + n_ch, g_o0 + n_ch, src=d_m, G0=t_groups)
    t_groups += 4 * TT
    norm_stage("n2", d_mix, 3 * D, 4 * D, a["g_pre_ffn"], t_groups, False, residual=a["x"])
    t_groups += 4 * TT
    project_stage("pq", a["w_pq"], d_q, c_o0 + 2 * n_ch, g_o0 + 2 * n_ch)
    main_scope.close()

    route_sb = (sb(stack, "idx_all", [P, TT * SLOTS + TOPK], U32), sb(stack, "wt_all", [P, TT * SLOTS]))
    lk = link(None, "dve")
    route(nc, a, stage, sem, sb, kc, ps, route_sb, d_q, lk)
    gather_experts(nc, a, stage, sem, sb, ps, route_sb, d_mod, d_x2, d_h2, lk, store_gate, range(TT))


def route(nc, a, stage, sem, sb, kc, ps, route_sb, d_q, lk):
    idx_all, wt_all = route_sb
    ident = kc[:, K_ID:K_ID + P]
    NH = 2 * PH
    with stage() as (st, block):
        qt = sb(st, "qt", [P, NH, P])
        q_t = sb(st, "q_t", [P, NH, P])
        keys = sb(st, "keys_sb", [P, 2, NKEY])
        sc = sb(st, "sc", [P, NH, NKEY])
        top = sb(st, "top", [P, NH, TOPK])
        topi = sb(st, "topi", [P, NH, TOPK], U32)
        topf = sb(st, "topf", [P, NH, TOPK])
        cand = sb(st, "cand", [P, PH, TOPK * TOPK])
        best = sb(st, "best", [P, PH, TOPK])
        pos = sb(st, "pos", [P, PH, TOPK], U32)
        pij = sb(st, "pij", [P, 2, PH, TOPK], U32)
        pf = sb(st, "pf", [P, 2, PH, TOPK])
        hot = sb(st, "hot", [P, 2, PH, TOPK, TOPK])
        sel = sb(st, "sel", [P, 2, PH, TOPK])
        idf = sb(st, "idf", [P, PH, TOPK])
        ex_t = sb(st, "ex_t", [P, 2, PH, TOPK])
        den = sb(st, "den", [P, 2, PH])
        s_q, s_keys, q_turned, q_taken = sem("r_q"), sem("r_keys"), sem("r_turned"), sem("r_taken")
        q_free = sem("r_qfree")
        sc_ready, sc_copied, sc_free = sem("r_scready"), sem("r_sccopied"), sem("r_scfree")
        s_ex, s_exd = sem("r_ex"), sem("r_exd")
        gate = sem("r_gate")

        @block.sync
        def _(sp):
            sp.dma_start(keys[:], a["keys"]).then_inc(s_keys, 16)
            with sp.Fori(0, TT) as t:
                sp.wait_ge(q_taken, t * 4 + 4)
                sp.dma_start(qt[:], d_q[bass.ds(t * P, P), :].rearrange("p (j n) -> p j n", j=NH)).then_inc(s_q, 16)

        @block.tensor
        def _(pe):
            pe.wait_ge(s_keys, 16)
            with pe.Fori(0, TT) as t:
                pe.wait_ge(s_q, t * 16 + 16)
                for g in range(4):
                    pe.wait_ge(q_taken, t * 4 + (g + 1))
                    for j in range(4):
                        mm = pe.transpose(ps[:, 4 + g, j * P:(j + 1) * P], qt[:, 4 * g + j], ident)
                    mm.then_inc(q_turned, 1)
                pe.wait_ge(sc_copied, t * 4 + 4)
                for g in range(4):
                    pe.wait_ge(q_taken, t * 4 + (g + 5))
                    for j in range(4):
                        mm = pe.matmul(ps[:, g, j * P:(j + 1) * P], q_t[:, 4 * g + j], keys[:, j % 2], start=True,
                                       stop=True)
                    mm.then_inc(sc_ready, 1)

        @block.scalar
        def _(act):
            act.sem_inc(q_taken, 4)
            act.sem_inc(sc_copied, 4)
            with act.Fori(0, TT) as t:
                for g in range(4):
                    act.wait_ge(q_turned, t * 4 + (g + 1))
                    if g == 0:
                        act.wait_ge(sc_copied, t * 4 + 4)
                    act.activation(q_t[:, 4 * g:4 * g + 4], ps[:, 4 + g].rearrange("p (j n) -> p j n", j=4),
                                   ACT.Copy).then_inc(q_taken, 1)
                act.wait_ge(sc_free, t + 1)
                for g in range(4):
                    act.wait_ge(sc_ready, t * 4 + (g + 1))
                    act.activation(sc[:, 4 * g:4 * g + 4], ps[:, g].rearrange("p (j n) -> p j n", j=4),
                                   ACT.Copy).then_inc(sc_copied, 1)
                act.wait_ge(s_ex, t + 1)
                act.activation(ex_t[:, 1], ex_t[:, 0], ACT.Exp).then_inc(s_exd, 1)

        @block.vector
        def _(dve):
            lk.eng = dve
            dve.sem_inc(sc_free, 1)
            lk.mark(dve.memset(idx_all[:, TT * SLOTS:], 0))

            def settle():
                lk.sync()
                dve.sem_inc(gate, 1)

            def top16(n, values, best, where):
                for r in range(2):
                    eight = slice(8 * r, 8 * r + 8)
                    settle()
                    for j in range(n):
                        lk.mark(dve.max(best(j)[:, eight], values(j)))
                    settle()
                    for j in range(n):
                        lk.mark(dve.max_index(where(j)[:, eight], best(j)[:, eight], values(j)))
                    if r == 0:
                        settle()
                        for j in range(n):
                            lk.mark(dve.match_replace(values(j), best(j)[:, eight], values(j), -3.0e38))
                lk.sync()

            with dve.Fori(0, TT) as t:
                lk.enter(t, 5 * NH + 5 * PH + 17)
                dve.wait_ge(sc_copied, t * 4 + 8)
                top16(NH, lambda j: sc[:, j], lambda j: top[:, j], lambda j: topi[:, j])
                dve.sem_inc(sc_free, 1)
                lk.mark(dve.tensor_copy(topf[:], topi[:]))
                pairs = top[:].rearrange("p (h two) k -> p h two k", two=2)
                at_i = [P, PH, TOPK, TOPK]
                lk.mark(dve.tensor_tensor(cand[:].rearrange("p h (i j) -> p h i j", i=TOPK),
                                          pairs[:, :, 0].unsqueeze(3).broadcast_to(at_i),
                                          pairs[:, :, 1].unsqueeze(2).broadcast_to(at_i), ALU.add))
                lk.sync()
                top16(PH, lambda h: cand[:, h], lambda h: best[:, h], lambda h: pos[:, h])
                lk.mark(dve.tensor_tensor(ex_t[:, 0], best[:], best[:, :, 0:1].broadcast_to([P, PH, TOPK]),
                                          ALU.subtract))
                lk.sync()
                dve.sem_inc(s_ex, 1)
                lk.mark(dve.tensor_scalar(pij[:, 0], pos[:], 4, None, ALU.logical_shift_right))
                lk.mark(dve.tensor_scalar(pij[:, 1], pos[:], TOPK - 1, None, ALU.bitwise_and))
                lk.sync()
                lk.mark(dve.tensor_copy(pf[:], pij[:]))
                lk.sync()
                number = kc[:, K_IOTA:K_IOTA + TOPK].unsqueeze(1).unsqueeze(1).broadcast_to([P, PH, TOPK, TOPK])
                keyf = topf[:].rearrange("p (h two) k -> p h two k", two=2)
                for n in range(2):
                    lk.mark(dve.tensor_tensor(hot[:, n], pf[:, n].unsqueeze(3).broadcast_to([P, PH, TOPK, TOPK]),
                                              number, ALU.is_equal))
                for n in range(2):
                    lk.sync(back=1)
                    lk.mark(dve.tensor_tensor(hot[:, n], hot[:, n],
                                              keyf[:, :, n].unsqueeze(2).broadcast_to([P, PH, TOPK, TOPK]), ALU.mult))
                for n in range(2):
                    lk.sync(back=1)
                    lk.mark(dve.tensor_reduce(sel[:, n], hot[:, n], AX.X, ALU.add))
                lk.sync()
                lk.mark(dve.scalar_tensor_tensor(out=idf[:], in0=sel[:, 0], scalar=float(NKEY), in1=sel[:, 1],
                                                 op0=ALU.mult, op1=ALU.add))
                lk.sync()
                lk.mark(dve.tensor_copy(idx_all[:, bass.ds(t * SLOTS, SLOTS)],
                                        idf[:].rearrange("p h k -> p (h k)")))
                dve.wait_ge(s_exd, t + 1)
                lk.mark(dve.tensor_reduce(den[:, 0], ex_t[:, 1], AX.X, ALU.add))
                lk.sync()
                lk.mark(dve.reciprocal(den[:, 1], den[:, 0]))
                lk.sync()
                lk.mark(dve.tensor_tensor(wt_all[:, bass.ds(t * SLOTS, SLOTS)].rearrange("p (h k) -> p h k", h=PH),
                                          ex_t[:, 1], den[:, 1].unsqueeze(2).broadcast_to([P, PH, TOPK]), ALU.mult))
                lk.leave_step()
            lk.leave(TT)


def gather_experts(nc, a, stage, sem, sb, ps, route_sb, d_mod, d_x2, d_h2, lk, gate, tiles):
    idx_all, wt_all = route_sb
    RING = 8
    NB = 4
    NT = len(tiles)
    t0 = tiles[0]
    with stage() as (st, block):
        u_ring = sb(st, "u_ring", [P, RING, D])
        v_ring = sb(st, "v_ring", [P, RING, D])
        h_t = sb(st, "h_t", [P, D])
        x_t = sb(st, "x_t", [P, D])
        acc = sb(st, "acc_f", [P, 2, D])
        idx16 = sb(st, "idx16", [P, 2, TOPK], U32)
        dots = sb(st, "dots", [P, 2, TOPK])
        gel = sb(st, "gel", [P, 2, TOPK])
        coef = sb(st, "coef", [P, 2, TOPK])
        post = sb(st, "f_post", [NSEQ, D])
        gp = sb(st, "f_gp", [NSEQ, D])
        rowsel = sb(st, "f_rowsel", [NSEQ, P])
        ss = sb(st, "f_ss", [P, 4])
        u_in = [sem(f"u_in{n}") for n in range(RING)]
        v_in = [sem(f"v_in{n}") for n in range(RING)]
        u_used, v_used = sem("u_used"), sem("v_used")
        idx_ready = sem("idx_ready")
        dotted, gelled = sem("dotted"), sem("gelled")
        s_h, s_xf, h_free, x_free = sem("s_h"), sem("s_xf"), sem("h_free"), sem("x_free")
        s_fmod, s_post, f_ready, f_used, s_fms, s_fsd, y_done, s_y = (
            sem("f_" + n) for n in ("mod", "post", "ready", "used", "ms", "sd", "done", "y"))
        dve_gate = sem("dve_gate")
        coef_ready = sem("coef_ready")
        per_head = TOPK // RING

        @block.sync
        def _(sp):
            sp.dma_start(post[:], d_mod[:, 5 * D:6 * D]).then_inc(s_fmod, 16)
            sp.dma_start(gp[:], a["g_post_ffn"].broadcast_to([NSEQ, D])).then_inc(s_fmod, 16)
            with sp.Fori(0, NT) as n:
                sp.wait_ge(h_free, n + 1)
                sp.dma_start(h_t[:], d_h2[bass.ds(n * P + t0 * P, P), :]).then_inc(s_h, 16)
                sp.wait_ge(x_free, n + 1)
                sp.dma_start(x_t[:], d_x2[bass.ds(n * P + t0 * P, P), :]).then_inc(s_xf, 16)
                sp.dma_start(rowsel[:], a["spread"][:, bass.ds(n * P + t0 * P, P)]).then_inc(s_xf, 16)

        @block.gpsimd
        def _(pool):
            with pool.Fori(0, NT) as n:
                with pool.Fori(0, PH // 2) as hh:
                    for b in range(2):
                        head = n * PH + (hh * 2 + b)
                        for s in range(TOPK):
                            r = s % RING
                            if s == 0:
                                pool.wait_ge(idx_ready, head + 1)
                            pool.wait_ge(u_used, head * TOPK + (s + 1))
                            pool.sem_inc(gate, 1)
                            pool.indirect_dma_start(
                                out=u_ring[:, r], out_offset=None, in_=a["u_exp"],
                                in_offset=bass.IndirectOffsetOnAxis(ap=idx16[:, b, s:s + 1], axis=0)
                            ).then_inc(u_in[r], 16)
                            pool.wait_ge(v_used, head * TOPK + (s + 1))
                            pool.sem_inc(gate, 1)
                            pool.indirect_dma_start(
                                out=v_ring[:, r], out_offset=None, in_=a["v_exp"],
                                in_offset=bass.IndirectOffsetOnAxis(ap=idx16[:, b, s:s + 1], axis=0)
                            ).then_inc(v_in[r], 16)

        @block.scalar
        def _(act):
            act.sem_inc(x_free, 1)
            with act.Fori(0, NT) as n:
                with act.Fori(0, PH // 2) as hh:
                    for b in range(2):
                        head = n * PH + (hh * 2 + b)
                        for k in range(TOPK // NB):
                            cols = slice(k * NB, (k + 1) * NB)
                            act.wait_ge(dotted, head * (TOPK // NB) + (k + 1))
                            act.activation(gel[:, b, cols], dots[:, b, cols], ACT.Gelu).then_inc(gelled, 1)
                act.wait_ge(s_fms, n + 1)
                act.activation(ss[:, 2:3], ss[:, 1:2], ACT.Sqrt).then_inc(s_fsd, 1)
                act.wait_ge(y_done, n + 1)
                act.dma_start(a["out_y"][bass.ds(n * P + t0 * P, P), :], x_t[:]).then_inc(s_y, 16)
                act.wait_ge(s_y, n * 16 + 16)
                act.sem_inc(x_free, 1)

        @block.tensor
        def _(pe):
            pe.wait_ge(s_post, 1)
            with pe.Fori(0, NT) as n:
                pe.wait_ge(s_xf, n * 32 + 32)
                pe.wait_ge(f_used, n * 4 + 4)
                for g in range(4):
                    pe.matmul(ps[:, g], rowsel[:], post[:, g * NCOL:(g + 1) * NCOL], start=True,
                              stop=True).then_inc(f_ready, 1)

        @block.vector
        def _(dve):
            lk.eng = dve
            dve.sem_inc(u_used, RING)
            dve.sem_inc(v_used, RING)
            dve.sem_inc(f_used, 4)
            dve.sem_inc(h_free, 1)
            dve.wait_ge(s_fmod, 32)
            dve.tensor_tensor(post[:], post[:], gp[:], ALU.mult).then_inc(s_post, 1)

            def copy_idx(gh, b):
                dve.tensor_copy(idx16[:, b], idx_all[:, bass.ds(gh * TOPK + t0 * SLOTS, TOPK)]).then_inc(idx_ready, 1)

            def dot_batch(n, head, b, k):
                base = n * (PH * per_head)
                for s in range(k * NB, (k + 1) * NB):
                    r = s % RING
                    dve.wait_ge(u_in[r], (base + head * per_head) * 16 + (s // RING * 16 + 16))
                    dve.scalar_tensor_tensor(out=u_ring[:, r], in0=u_ring[:, r], scalar=1.0, in1=h_t[:],
                                             op0=ALU.mult, op1=ALU.mult,
                                             accum_out=dots[:, b, s:s + 1]).then_inc(u_used, 1)
                dve.wait_ge(u_used, (n * PH + head) * TOPK + ((k + 1) * NB + RING))
                dve.sem_inc(dotted, 1)

            def add_batch(n, head, b, k):
                base = n * (PH * per_head)
                cols = slice(k * NB, (k + 1) * NB)
                dve.wait_ge(gelled, (n * PH + head) * (TOPK // NB) + (k + 1))
                dve.tensor_tensor(coef[:, b, cols], gel[:, b, cols],
                                  wt_all[:, bass.ds((n * PH + head) * TOPK + (k * NB + t0 * SLOTS), NB)],
                                  ALU.mult).then_inc(coef_ready, 1)
                dve.wait_ge(coef_ready, (n * PH + head) * (TOPK // NB) + (k + 1))
                for s in range(k * NB, (k + 1) * NB):
                    r = s % RING
                    dve.wait_ge(v_in[r], (base + head * per_head) * 16 + (s // RING * 16 + 16))
                    dve.wait_ge(v_used, (n * PH + head) * TOPK + (s + RING - 1))
                    dve.scalar_tensor_tensor(out=acc[:, s % 2], in0=v_ring[:, r], scalar=coef[:, b, s:s + 1],
                                             in1=acc[:, s % 2], op0=ALU.mult, op1=ALU.add).then_inc(v_used, 1)

            copy_idx(0, 0)
            with dve.Fori(0, NT) as n:
                lk.enter(n, 4)
                dve.wait_ge(s_h, n * 16 + 16)
                lk.mark(dve.memset(acc[:], 0.0))
                lk.sync()
                dve.sem_inc(dve_gate, 1)
                with dve.Fori(0, PH // 2) as hh:
                    for b in range(2):
                        head = hh * 2 + b
                        copy_idx(n * PH + (head + 1), 1 - b)
                        dot_batch(n, head, b, 0)
                        for k in range(1, TOPK // NB):
                            dot_batch(n, head, b, k)
                            add_batch(n, head, b, k - 1)
                        add_batch(n, head, b, TOPK // NB - 1)
                dve.sem_inc(h_free, 1)
                dve.wait_ge(v_used, (n + 1) * PH * TOPK + RING)
                lk.mark(dve.tensor_tensor(acc[:, 0], acc[:, 0], acc[:, 1], ALU.add))
                lk.sync()
                lk.mark(dve.scalar_tensor_tensor(out=acc[:, 1], in0=acc[:, 0], scalar=1.0, in1=acc[:, 0],
                                                 op0=ALU.mult, op1=ALU.mult, accum_out=ss[:, 0:1]))
                lk.sync()
                dve.tensor_scalar(ss[:, 1:2], ss[:, 0:1], 1.0 / D, EPS, ALU.mult, ALU.add).then_inc(s_fms, 1)
                dve.wait_ge(s_fsd, n + 1)
                lk.mark(dve.reciprocal(ss[:, 3:4], ss[:, 2:3]))
                lk.sync()
                for g in range(4):
                    cols = slice(g * NCOL, (g + 1) * NCOL)
                    dve.wait_ge(f_ready, n * 4 + (g + 1))
                    dve.scalar_tensor_tensor(out=acc[:, 0, cols], in0=acc[:, 0, cols], scalar=ss[:, 3:4],
                                             in1=ps[:, g], op0=ALU.mult, op1=ALU.mult).then_inc(f_used, 1)
                dve.wait_ge(f_used, n * 4 + 8)
                dve.wait_ge(s_xf, n * 32 + 32)
                dve.tensor_tensor(x_t[:], x_t[:], acc[:, 0], ALU.add).then_inc(y_done, 1)
                dve.wait_ge(y_done, n + 1)
                dve.sem_inc(dve_gate, 1)
                lk.leave_step()
            lk.leave(NT)


def layout(inp):
    f = {k: np.asarray(v) for k, v in inp.items()}
    k, spread = constants()
    c = np.concatenate([f["c_prompt"], f["c_sample"]], 0)
    return {
        "x": np.concatenate([f["x_prompt"].reshape(NP_TOK, D), f["x_sample"].reshape(NTOK - NP_TOK, D)], 0),
        "cT": np.ascontiguousarray(c.T.reshape(KD, P, NSEQ).transpose(1, 0, 2)),
        "w_ada": f["w_ada"][0], "b_ada": f["b_ada"],
        "consts": k, "spread": spread,
        "g_pre_mix": f["g_pre_mix"],
        "w_in": f["w_in"][0],
        "g_gla_out": f["g_gla_out"],
        "g_post_mix": f["g_post_mix"], "g_pre_ffn": f["g_pre_ffn"], "g_post_ffn": f["g_post_ffn"],
        "taps": np.concatenate([f["w_dw"][0].T, f["b_dw"].T], 1),
        "cacheT": np.ascontiguousarray(f["cache_conv"][0].transpose(2, 0, 1)),
        "cache": f["cache_conv"][0],
        "lnp": np.stack([f["g_conv_ln"][0].reshape(CT, P).T, f["b_conv_ln"][0].reshape(CT, P).T], 1),
        "w_conv_o": f["w_conv_o"][0], "w_gla_o": f["w_gla_o"][0], "w_out": f["w_out"][0], "w_pq": f["w_pq"][0],
        "state": f["state_gla"].reshape(STREAMS, DK, DVH),
        "w_alpha": np.concatenate([f["w_alpha_up"][0], f["b_alpha"]], 0),
        "keys": np.stack([f["k_sub1"][0].T, f["k_sub2"][0].T], 1),
        "u_exp": f["u_exp"][0], "v_exp": f["v_exp"][0],
    }


OUTS = {
    "out_y": (NTOK, D),
    "out_sp": (DK, DVH), "out_cp": (HIST, CC),
    "out_ss": (STREAMS, DK, DVH), "out_cs": (STREAMS, HIST, CC),
}


def kernel(**inputs):
    import concourse.bacc as bacc
    from concourse.bass_utils import run_bass_kernel_spmd

    arrays = {name: np.ascontiguousarray(value) for name, value in layout(inputs).items()}
    nc = bacc.Bacc("TRN2", target_bir_lowering=False, num_devices=1)
    a = {}
    for name, value in arrays.items():
        a[name] = nc.dram_tensor(name, value.shape, mybir.dt.from_np(value.dtype), kind="ExternalInput").ap()
    for name, shape in OUTS.items():
        a[name] = nc.dram_tensor(name, shape, F32, kind="ExternalOutput").ap()
    build(nc, a)
    nc.finalize()
    got = run_bass_kernel_spmd(nc, [arrays], core_ids=[0]).results[0]
    return (got["out_y"][:NP_TOK].reshape(1, NP_TOK, D),
            got["out_y"][NP_TOK:].reshape(STREAMS, ST_TOK, D),
            got["out_sp"].reshape(1, 1, HEADS, DKH, DVH),
            got["out_cp"].reshape(1, 1, HIST, CC),
            got["out_ss"].reshape(1, STREAMS, HEADS, DKH, DVH),
            got["out_cs"].reshape(1, STREAMS, HIST, CC))
```
